# Optimizing a Trainium2 kernel written in Bass

```python
import math
import jax, jax.numpy as jnp
from jax import lax
import numpy as np

D_MODEL = 1024
BATCH = 1
SEQ = 512
DEPTH = 2

CHUNK = 64
Q_BLOCK = 128
N_HEADS = 8
QK_NOPE_DIM = 128
QK_ROPE_DIM = 64
V_HEAD_DIM = 128
Q_LORA_RANK = 512
KV_LORA_RANK = 256
ROPE_THETA = 10000.0
MAX_POS_OFFSET = 16384
CONV_WIDTH = 3
D_FF = ((8 * D_MODEL // 3 + 255) // 256) * 256
RMS_EPS = 1e-6
N_MLA_LAYERS = (DEPTH + 1) // 2
N_CONV_LAYERS = DEPTH // 2
MLA_IN_DIM = Q_LORA_RANK + KV_LORA_RANK + QK_ROPE_DIM

kernel_name = "hybrid_mla_shortconv_swiglu_trunk"

def rms_norm(x, g):
    xf = x.astype(jnp.float32)
    y = xf * lax.rsqrt(jnp.mean(xf * xf, axis=-1, keepdims=True) + RMS_EPS)
    return (y * g.astype(jnp.float32)).astype(x.dtype)

def rope_tables(positions):
    inv_freq = 1.0 / (ROPE_THETA ** (jnp.arange(0, QK_ROPE_DIM, 2, dtype=jnp.float32) / QK_ROPE_DIM))
    ang = positions.astype(jnp.float32)[..., None] * inv_freq
    return jnp.cos(ang), jnp.sin(ang)

def apply_rope(x, cos, sin):
    xf = x.astype(jnp.float32)
    x1, x2 = jnp.split(xf, 2, axis=-1)
    out = jnp.concatenate([x1 * cos - x2 * sin, x1 * sin + x2 * cos], axis=-1)
    return out.astype(x.dtype)

def chunk_causal_mla_attention(q_n, q_r, k_n, k_r, v):
    bsz, seq, h, _ = q_n.shape
    nb = seq // Q_BLOCK
    scale = 1.0 / math.sqrt(QK_NOPE_DIM + QK_ROPE_DIM)
    qn_b = q_n.reshape(bsz, nb, Q_BLOCK, h, QK_NOPE_DIM).transpose(1, 0, 2, 3, 4)
    qr_b = q_r.reshape(bsz, nb, Q_BLOCK, h, QK_ROPE_DIM).transpose(1, 0, 2, 3, 4)
    k_chunk = jnp.arange(seq) // CHUNK

    def one_block(args):
        qn, qr, blk = args
        q_chunk = (blk * Q_BLOCK + jnp.arange(Q_BLOCK)) // CHUNK
        s = (jnp.einsum('bqhd,bkhd->bhqk', qn, k_n).astype(jnp.float32)
             + jnp.einsum('bqhd,bkd->bhqk', qr, k_r).astype(jnp.float32)) * scale
        mask = k_chunk[None, :] <= q_chunk[:, None]
        s = jnp.where(mask[None, None], s, jnp.float32(-1e30))
        p = jax.nn.softmax(s, axis=-1).astype(v.dtype)
        return jnp.einsum('bhqk,bkhd->bqhd', p, v)

    out = lax.map(one_block, (qn_b, qr_b, jnp.arange(nb)))
    return out.transpose(1, 0, 2, 3, 4).reshape(bsz, seq, h, V_HEAD_DIM)

def mla_mixer(h, positions, w_in, g_cq, g_ckv, w_uq, w_ukv, w_o):
    bsz, seq, _ = h.shape
    proj = h @ w_in
    c_q = proj[..., :Q_LORA_RANK]
    c_kv = proj[..., Q_LORA_RANK:Q_LORA_RANK + KV_LORA_RANK]
    k_r = proj[..., Q_LORA_RANK + KV_LORA_RANK:]
    c_q = rms_norm(c_q, g_cq)
    c_kv = rms_norm(c_kv, g_ckv)
    q = (c_q @ w_uq).reshape(bsz, seq, N_HEADS, QK_NOPE_DIM + QK_ROPE_DIM)
    q_n, q_r = q[..., :QK_NOPE_DIM], q[..., QK_NOPE_DIM:]
    kv = (c_kv @ w_ukv).reshape(bsz, seq, N_HEADS, QK_NOPE_DIM + V_HEAD_DIM)
    k_n, v = kv[..., :QK_NOPE_DIM], kv[..., QK_NOPE_DIM:]
    cos, sin = rope_tables(positions)
    q_r = apply_rope(q_r, cos[:, :, None, :], sin[:, :, None, :])
    k_r = apply_rope(k_r, cos, sin)
    attn = chunk_causal_mla_attention(q_n, q_r, k_n, k_r, v)
    return attn.reshape(bsz, seq, N_HEADS * V_HEAD_DIM) @ w_o

def short_conv_mixer(h, w_in, conv_w, w_out):
    bcx = h @ w_in
    b_gate = bcx[..., :D_MODEL]
    c_gate = bcx[..., D_MODEL:2 * D_MODEL]
    xp = bcx[..., 2 * D_MODEL:]
    u = c_gate * xp
    u_conv = lax.conv_general_dilated(
        u, conv_w[:, None, :].astype(u.dtype), window_strides=(1,),
        padding=[(CONV_WIDTH - 1, 0)], dimension_numbers=('NWC', 'WIO', 'NWC'),
        feature_group_count=D_MODEL)
    return (b_gate * u_conv) @ w_out

def swiglu(h, w_gate, w_up, w_down):
    return (jax.nn.silu(h @ w_gate) * (h @ w_up)) @ w_down

def setup_inputs(seed: int = 0) -> dict:
    key = jax.random.key(seed)
    ks = jax.random.split(key, 24)

    def w(k, shape, fan_in):
        return jax.random.normal(k, shape, jnp.float32) * (fan_in ** -0.5)

    def gain(k, shape):
        return 1.0 + 0.05 * jax.random.normal(k, shape, jnp.float32)

    x = jax.random.normal(ks[0], (BATCH, SEQ, D_MODEL), jnp.float32)
    offset = jax.random.randint(ks[1], (BATCH, 1), 0, MAX_POS_OFFSET, dtype=jnp.int32)
    positions = (offset + jnp.arange(SEQ, dtype=jnp.int32)[None, :]).astype(jnp.int32)
    L_a, L_b = N_MLA_LAYERS, N_CONV_LAYERS
    return {
        "x": x,
        "positions": positions,
        "mla_norm": gain(ks[2], (L_a, D_MODEL)),
        "mla_w_in": w(ks[3], (L_a, D_MODEL, MLA_IN_DIM), D_MODEL),
        "mla_g_cq": gain(ks[4], (L_a, Q_LORA_RANK)),
        "mla_g_ckv": gain(ks[5], (L_a, KV_LORA_RANK)),
        "mla_w_uq": w(ks[6], (L_a, Q_LORA_RANK, N_HEADS * (QK_NOPE_DIM + QK_ROPE_DIM)), Q_LORA_RANK),
        "mla_w_ukv": w(ks[7], (L_a, KV_LORA_RANK, N_HEADS * (QK_NOPE_DIM + V_HEAD_DIM)), KV_LORA_RANK),
        "mla_w_o": w(ks[8], (L_a, N_HEADS * V_HEAD_DIM, D_MODEL), N_HEADS * V_HEAD_DIM),
        "conv_norm": gain(ks[9], (L_b, D_MODEL)),
        "conv_w_in": w(ks[10], (L_b, D_MODEL, 3 * D_MODEL), D_MODEL),
        "conv_w": w(ks[11], (L_b, CONV_WIDTH, D_MODEL), CONV_WIDTH),
        "conv_w_out": w(ks[12], (L_b, D_MODEL, D_MODEL), D_MODEL),
        "ffn_norm": gain(ks[13], (DEPTH, D_MODEL)),
        "ffn_w_gate": w(ks[14], (DEPTH, D_MODEL, D_FF), D_MODEL),
        "ffn_w_up": w(ks[15], (DEPTH, D_MODEL, D_FF), D_MODEL),
        "ffn_w_down": w(ks[16], (DEPTH, D_FF, D_MODEL), D_FF),
        "final_norm": gain(ks[17], (D_MODEL,)),
    }

def reference(x, positions, mla_norm, mla_w_in, mla_g_cq, mla_g_ckv, mla_w_uq,
              mla_w_ukv, mla_w_o, conv_norm, conv_w_in, conv_w, conv_w_out,
              ffn_norm, ffn_w_gate, ffn_w_up, ffn_w_down, final_norm):
    h = x
    for i in range(DEPTH):
        j = i // 2
        if i % 2 == 0:
            h = h + mla_mixer(rms_norm(h, mla_norm[j]), positions, mla_w_in[j],
                              mla_g_cq[j], mla_g_ckv[j], mla_w_uq[j], mla_w_ukv[j], mla_w_o[j])
        else:
            h = h + short_conv_mixer(rms_norm(h, conv_norm[j]), conv_w_in[j],
                                     conv_w[j], conv_w_out[j])
        h = h + swiglu(rms_norm(h, ffn_norm[i]), ffn_w_gate[i], ffn_w_up[i], ffn_w_down[i])
    return rms_norm(h, final_norm)


_drawn_inputs = setup_inputs


def setup_inputs(seed=0):
    import zlib

    import numpy as np

    out = dict(_drawn_inputs(seed))
    spreads = {}
    factors = {'mla_norm': 3.256,
     'mla_g_cq': 5.611,
     'mla_g_ckv': 3.639,
     'ffn_norm': 3.196,
     'conv_norm': 4.398}
    for name, (base, spread) in spreads.items():
        noise = np.random.default_rng([zlib.crc32(name.encode()), seed]).standard_normal(out[name].shape)
        drawn = base * np.exp(spread * noise) if base else spread * noise
        out[name] = __import__('jax').numpy.asarray(drawn.astype(out[name].dtype))
    for name, factor in factors.items():
        out[name] = (out[name] * factor).astype(out[name].dtype)
    return out
```

```python
from collections import Counter
from contextlib import ExitStack, contextmanager
import math

import numpy as np

import concourse.bass as bass
from concourse import mybir

F32 = mybir.dt.float32
F32R = mybir.dt.float32r
I32 = mybir.dt.int32
ALU = mybir.AluOpType
ACT = mybir.ActivationFunctionType
AX_X = mybir.AxisListType.X
ds = bass.ds

P = 128
SEQ = 512
TOK = SEQ // P
D = 1024
KD = D // P
HEADS, NOPE, ROPE, VDIM = 8, 128, 64, 128
QRANK, KVRANK = 512, 256
KQ, KKV = QRANK // P, KVRANK // P
D_FF = (8 * D // 3 + 255) // 256 * 256
KF = D_FF // P
CONV = 3
EPS = 1e-6
SCALE = 1.0 / math.sqrt(NOPE + ROPE)
HALF = ROPE // 2
SLOT = KD * 2 * P
PAIRS = HEADS // 2
DOWN_K = [range(0, 8), range(8, 16), range(16, KF)]
UQ_N = KQ * 2 * (NOPE + ROPE)
UKV_N = KKV * 2 * (NOPE + VDIM)
KR_N = KD * 2 * ROPE
DOWN_N = [len(ks) * 2 * P for ks in DOWN_K]
DOWN_AHEAD = (DOWN_N * 3)[2:8]

VEC_ROWS = [("mla_norm", KD), ("mla_g_cq", KQ), ("mla_g_ckv", KKV), ("ffn_norm0", KD), ("conv_norm", KD),
            ("ffn_norm1", KD), ("final_norm", KD), ("conv_w", CONV * KD)]
VEC = {}
for _name, _rows in VEC_ROWS:
    VEC[_name] = sum(r for _, r in VEC_ROWS[:len(VEC)])
N_VEC = sum(r for _, r in VEC_ROWS)
FREQ, SIGN = N_VEC, N_VEC + 1

PT_STEP = 3 * P
QN, QR = 0, 2 * SEQ
KN = QR + SEQ
VV = KN + 2 * SEQ
PT = [VV + TOK * 2 * VDIM, VV + TOK * 2 * VDIM + TOK * PT_STEP + P]
OO = PT[1] + TOK * PT_STEP + P
MASK_Q = OO + HEADS * SEQ
MASK_K = MASK_Q + P
assert MASK_K + P <= KF * SEQ
PI_BELOW = 3.1415925
ROUND = 1.5 * 2.0 ** 23
MASKED = -float(2.0 ** 93)

PROB = [[h * 1280 + x for x in (0, 128, 384, 768)] for h in range(2)]


def two_pi_parts():
    rest, parts = 2 * math.pi, []
    for _ in range(2):
        exponent = math.floor(math.log2(rest))
        unit = 2.0 ** (exponent - 11)
        parts.append(math.floor(rest / unit) * unit)
        rest -= parts[-1]
    return parts + [rest]


class Tally:

    def __init__(self):
        self.base, self.here, self.per, self.i = Counter(), Counter(), {}, None

    def add(self, name, k=1):
        self.here[name] += k
        return self.now(name)

    def now(self, name):
        n = self.base[name] + self.here[name]
        per = self.per.get(name, 0)
        return n if self.i is None or not per else self.i * per + n

    @contextmanager
    def loop(self, engine, rounds, **per):
        self.base, self.here = self.base + self.here, Counter()
        with engine.Fori(0, rounds) as i:
            self.per, self.i = per, i
            yield i
            assert dict(+self.here) == per, (dict(self.here), per)
        self.base += Counter({k: v * rounds for k, v in per.items()})
        self.here, self.per, self.i = Counter(), {}, None


def wait(engine, semaphore, count):
    if not (isinstance(count, int) and count == 0):
        engine.wait_ge(semaphore, count)


def turned_view(t, h, qi):
    c0 = PT[h] + qi * P
    return t[:, c0:c0 + TOK * PT_STEP].rearrange("p (j c) -> p j c", j=TOK)[:, 0:qi + 1, 0:P]


def build(nc, xt, positions, vectors, weights_in, out):
    with ExitStack() as ctx:
        def sb(name, cols, dt=F32):
            return ctx.enter_context(nc.sbuf_tensor(name, [P, cols], dt))

        def sem(name):
            return ctx.enter_context(nc.semaphore(name))

        xT = sb("xT", KD * SEQ)
        a_hi, a_lo = sb("a_hi", KD * SEQ, F32R), sb("a_lo", KD * SEQ, F32R)
        mid_hi, mid_lo = sb("mid_hi", KF * SEQ, F32R), sb("mid_lo", KF * SEQ, F32R)
        raw = [sb(f"raw{s}", SLOT) for s in range(2)]
        w_hi = [sb(f"w_hi{s}", SLOT, F32R) for s in range(2)]
        w_lo = [sb(f"w_lo{s}", SLOT, F32R) for s in range(2)]
        work = sb("work", 6 * SEQ)
        cos, sin = sb("cos", SEQ), sb("sin", SEQ)
        rstd = sb("rstd", SEQ)
        acc = sb("acc", SEQ)
        sq = sb("sq", SEQ)
        ident, ones = sb("ident", P), sb("ones", P)
        vec = sb("vec", N_VEC + 2)
        row_max, exp_bias, row_sum, row_inv = (sb(n, 8) for n in ("row_max", "exp_bias", "row_sum", "row_inv"))
        eps = sb("eps", 1)
        bank = [ctx.enter_context(nc.psum_tensor(f"bank{b}", [P, SEQ], F32)) for b in range(8)]
        A, MID = (a_hi, a_lo), (mid_hi, mid_lo)
        HEAD_OUT = tuple(t[:, OO:OO + HEADS * SEQ] for t in MID)

        def tile(t, m, n=SEQ):
            return t[:, m * SEQ:m * SEQ + n]

        def turned_bank(qi):
            return bank[4 + qi % 2][:, 0:(qi + 1) * P].rearrange("p (j c) -> p j c", c=P)

        x_loaded = [sem(f"x_loaded{j}") for j in range(KD // 2)]
        positions_loaded, vectors_loaded = sem("positions_loaded"), sem("vectors_loaded")
        raw_loaded = [sem(f"raw_loaded{s}") for s in range(2)]
        hi_split = [sem(f"hi_split{s}") for s in range(2)]
        w_split = [sem(f"w_split{s}") for s in range(2)]
        chunk_done = [sem(f"chunk_done{s}") for s in range(2)]
        drained = [sem(f"drained{b}") for b in range(8)]
        operand_ready = sem("operand_ready")
        hi_taken = sem("hi_taken")
        squares_added = sem("squares_added")
        stat_summed = sem("stat_summed")
        rms_done = sem("rms_done")
        silu_done = sem("silu_done")
        angles_ready, trig_done = sem("angles_ready"), sem("trig_done")
        masks_made, ones_made, ident_made = sem("masks_made"), sem("ones_made"), sem("ident_made")
        keys_done = sem("keys_done")
        rope_ready = sem("rope_ready")
        scores_done = sem("scores_done")
        max_ready = sem("max_ready")
        probs_ready = sem("probs_ready")
        probs_turned = sem("probs_turned")
        head_done = sem("head_done")
        y_ready = sem("y_ready")
        out_stored = sem("out_stored")
        step = sem("step")
        zeroed = sem("zeroed")

        block = ctx.enter_context(nc.Block())

        @block.sync
        def _(sp):
            T = Tally()
            for j in range(KD // 2):
                sp.dma_start(xT[:, 2 * j * SEQ:2 * (j + 1) * SEQ].rearrange("p (t s) -> p t s", t=2),
                             xt[2 * j * P:2 * (j + 1) * P, :].rearrange("(t p) s -> p t s", p=P)).then_inc(x_loaded[j], 16)

            def load(s, c, n=SLOT):
                wait(sp, w_split[s], T.add(f"slot{s}") - 1)
                sp.dma_start(raw[s][:, 0:n].rearrange("p (o n) -> p o n", o=1),
                             weights_in[ds(c, 1), :, 0:n].rearrange("o p n -> p o n")).then_inc(raw_loaded[s], 16)

            def loads(c0, rounds, sizes):
                per = len(sizes)
                with T.loop(sp, rounds, slot0=per // 2, slot1=per // 2) as i:
                    for k, n in enumerate(sizes):
                        load(k % 2, i * per + (c0 + k), n)
                return c0 + rounds * per

            c = 4
            for k, n in enumerate([SLOT, SLOT, SLOT, KR_N]):
                load(k % 2, k, n)
            c = loads(c, PAIRS, [UQ_N, UKV_N])
            c = loads(c, 2, [SLOT] * 2)
            for layer in range(2):
                c = loads(c, KF // 2, [SLOT] * 2)
                c = loads(c, 2, DOWN_N * 2)
                if layer == 0:
                    c = loads(c, 8, [SLOT] * 2)
            for m in range(KD):
                sp.wait_ge(y_ready, m + 1)
                sp.dma_start(out[m * P:(m + 1) * P, :], tile(xT, m)).then_inc(out_stored, 16)
            sp.wait_ge(out_stored, 16 * KD)

        @block.gpsimd
        def _(pool):
            pool.dma_start(tile(work, 5).bitcast(I32), positions.partition_broadcast(P)).then_inc(positions_loaded, 16)
            pool.dma_start(vec[:, :], vectors).then_inc(vectors_loaded, 16)
            pool.memset(ident[:, :], 0.0).then_inc(zeroed, 1)
            pool.wait_ge(zeroed, 1)
            pool.affine_select(out=ident[:, :], in_=ident[:, :], compare_op=ALU.not_equal, fill=1.0, base=0,
                               pattern=[[-1, P]], channel_multiplier=1).then_inc(ident_made, 1)

        @block.tensor
        def _(pe):
            T = Tally()

            def open_bank(b):
                wait(pe, drained[b], T.add(f"b{b}") - 1)

            def taken(b):
                pe.wait_ge(drained[b], T.now(f"b{b}"))

            def product(o, lhs, rhs, start, stop):
                pe.matmul(o, lhs[0], rhs[0], start=start, stop=False, skip_group_check=True)
                pe.matmul(o, lhs[0], rhs[1], start=False, stop=False, skip_group_check=True)
                return pe.matmul(o, lhs[1], rhs[0], start=False, stop=stop, skip_group_check=True)

            def slot(s, c0):
                return w_hi[s][:, c0:c0 + P], w_lo[s][:, c0:c0 + P]

            def operand(buf, k):
                return tile(buf[0], k), tile(buf[1], k)

            def chunk(s, banks, buf, ks=range(KD), first=True, last=True, ready=None):
                pe.wait_ge(w_split[s], T.add(f"slot{s}"))
                if first:
                    for b in banks:
                        open_bank(b)
                for n, k in enumerate(ks):
                    if ready is not None:
                        pe.wait_ge(operand_ready, ready + k + 1)
                    for m, b in enumerate(banks):
                        mm = product(bank[b][:, :], slot(s, (n * len(banks) + m) * P), operand(buf, k),
                                     first and n == 0, last and n == len(ks) - 1)
                mm.then_inc(chunk_done[s], 1)

            def stat(b, tiles):
                pe.wait_ge(squares_added, T.add("squares", tiles))
                open_bank(b)
                pe.matmul(bank[b][:, :], ones[:, :], acc[:, :], start=True, stop=True).then_inc(stat_summed, 1)

            pe.wait_ge(ones_made, 1)
            chunk(0, [0, 1], A, ready=0)
            stat(7, KD)
            chunk(1, [2, 3], A)
            chunk(0, [4, 5], A)
            stat(7, KQ)
            chunk(1, [6], A)
            stat(0, KKV)
            made = KD
            pe.wait_ge(masks_made, 1)
            pe.wait_ge(ident_made, 1)

            with T.loop(pe, PAIRS, slot0=1, slot1=1, b0=3, b1=3, b2=3, b3=3, b4=5, b5=5, b6=2, b7=1,
                        rope=1, scores=8, probs=8):
                chunk(0, [0, 1, 2], A, range(KQ), ready=made)
                pe.wait_ge(w_split[1], T.add("slot1"))
                pe.wait_ge(operand_ready, made + KQ + KKV)
                for h in range(2):
                    open_bank(3 + h)
                    for k in range(KKV):
                        mm = product(bank[3 + h][:, :], slot(1, (k * 4 + h) * P), operand(A, KQ + k), k == 0, k == KKV - 1)
                mm.then_inc(keys_done, 1)
                for j in range(TOK):
                    if j % 2 == 0:
                        open_bank(5 + j // 2)
                    o = bank[5 + j // 2][:, j % 2 * 2 * VDIM:(j % 2 + 1) * 2 * VDIM]
                    for k in range(KKV):
                        c = tuple(t[:, (KQ + k) * SEQ + j * P:(KQ + k) * SEQ + (j + 1) * P] for t in A)
                        wv = tuple(t[:, (k * 4 + 2) * P:(k * 4 + 4) * P] for t in (w_hi[1], w_lo[1]))
                        mm = product(o, c, wv, k == 0, k == KKV - 1)
                mm.then_inc(chunk_done[1], 1)
                values = [T.now("b5"), T.now("b6")]
                for h in range(2):
                    taken(h)
                    taken(3 + h)
                    if h == 0:
                        pe.wait_ge(rope_ready, T.add("rope"))
                        pe.wait_ge(operand_ready, made + KQ + KKV + 1)
                    for qi in range(TOK):
                        L = (qi + 1) * P
                        open_bank(qi)
                        o = bank[qi][:, 0:L]
                        qn = tuple(t[:, QN + h * SEQ + qi * P:QN + h * SEQ + (qi + 1) * P] for t in MID)
                        qr = tuple(t[:, QR + qi * P:QR + (qi + 1) * P] for t in MID)
                        product(o, qn, tuple(t[:, KN + h * SEQ:KN + h * SEQ + L] for t in MID), True, False)
                        product(o, qr, tuple(tile(t, KQ + KKV + h, L) for t in A), False, False)
                        pe.matmul(bank[qi][:, L - P:L], mid_hi[:, MASK_Q:MASK_Q + P], mid_hi[:, MASK_K:MASK_K + P],
                                  start=False, stop=True, skip_group_check=True).then_inc(scores_done, 1)
                        T.add("scores")
                turned = []
                for h in range(2):
                    for qi in range(TOK):
                        pe.wait_ge(probs_ready, T.add("probs"))
                        b = 4 + qi % 2
                        open_bank(b)
                        for j in range(qi + 1):
                            p0 = PROB[h][qi] + j * P
                            tr = pe.transpose(bank[b][:, j * P:(j + 1) * P], work[:, p0:p0 + P], ident[:, :])
                        tr.then_inc(probs_turned, 1)
                    turned.append((T.now("b4"), T.now("b5")))
                pe.wait_ge(drained[5], values[0])
                pe.wait_ge(drained[6], values[1])
                for h in range(2):
                    pe.wait_ge(drained[4], turned[h][0])
                    pe.wait_ge(drained[5], turned[h][1])
                    open_bank(6 + h)
                    for j in range(TOK):
                        v0, p0, n = VV + (j * 2 + h) * VDIM, PT[h] + j * SEQ, SEQ - j * P
                        mm = product(bank[6 + h][:, j * P:], tuple(t[:, v0:v0 + VDIM] for t in MID),
                                     tuple(t[:, p0:p0 + n] for t in MID), j == 0, j == TOK - 1)
                    mm.then_inc(head_done, 1)
            made += KQ + KKV + 1

            def two_pairs(buf, ready=None):
                with T.loop(pe, 2, slot0=1, slot1=1, b0=1, b1=1, b2=1, b3=1):
                    chunk(0, [0, 1], buf, ready=ready)
                    chunk(1, [2, 3], buf)

            def ffn(made):
                chunk(0, [0, 1], A, ready=made)
                stat(4, KD)
                chunk(1, [2, 3], A)
                with T.loop(pe, KF // 2 - 1, slot0=1, slot1=1, b0=1, b1=1, b2=1, b3=1):
                    chunk(0, [0, 1], A)
                    chunk(1, [2, 3], A)
                made += KD
                with T.loop(pe, 2, slot0=3, slot1=3, b4=1, b5=1, b6=1, b7=1):
                    for c in range(6):
                        pair = c // 3
                        chunk(c % 2, [4 + 2 * pair, 5 + 2 * pair], MID, DOWN_K[c % 3], c % 3 == 0, c % 3 == 2,
                              ready=made if pair == 0 else None)
                return made + KF

            taken(6)
            taken(7)
            two_pairs(HEAD_OUT)
            made = ffn(made)
            for c in range(12):
                chunk(c % 2, [2 * (c % 3), 2 * (c % 3) + 1], A, ready=made if c == 0 else None)
                if c == 0:
                    stat(6, KD)
            made += KD
            two_pairs(MID, made)
            made += KD
            made = ffn(made)
            stat(0, KD)

        @block.scalar
        def _(act):
            T = Tally()

            def split(s, n=SLOT):
                k = T.add(f"slot{s}")
                act.wait_ge(raw_loaded[s], k * 16)
                wait(act, chunk_done[s], k - 1)
                act.activation(w_hi[s][:, 0:n], raw[s][:, 0:n], ACT.Copy).then_inc(hi_split[s], 1)

            def rms(b, width):
                act.wait_ge(stat_summed, T.add("stat"))
                act.activation(bank[b][:, :], bank[b][:, :], ACT.Sqrt, bias=eps[:, 0:1], scale=1.0 / width).then_inc(rms_done, 1)

            T.add("b1")
            act.wait_ge(vectors_loaded, 16)
            act.wait_ge(angles_ready, 2)
            act.activation(sin[:, :], tile(work, 0), ACT.Sin, scale=vec[:, SIGN:SIGN + 1]).then_inc(trig_done, 1)
            act.activation(cos[:, :], tile(work, 1), ACT.Sin).then_inc(trig_done, 1)
            split(0)
            split(1)
            act.wait_ge(ones_made, 1)
            split(0)
            rms(7, D)
            split(1, KR_N)
            split(0, UQ_N)
            rms(7, QRANK)
            split(1, UKV_N)
            rms(0, KVRANK)

            def take(dst, src):
                act.activation(dst, src, ACT.Copy).then_inc(hi_taken, 1)

            def exps(h):
                for qi in range(TOK):
                    act.wait_ge(max_ready, T.add("max"))
                    k, L = h * TOK + qi, (qi + 1) * P
                    act.activation(work[:, PROB[h][qi]:PROB[h][qi] + L], bank[qi][:, 0:L], ACT.Exp,
                                   bias=exp_bias[:, k:k + 1], scale=SCALE, accum_out=row_sum[:, k:k + 1]).then_inc(drained[qi], 1)

            with T.loop(act, PAIRS, slot0=1, slot1=1, keys=1, max=8, turned=8, b1=3):
                T.add("b1", 3)
                act.wait_ge(chunk_done[0], T.now("slot0"))
                for h in range(2):
                    take(tile(mid_hi[:, QN:], h), bank[h][:, :])
                split(0)
                act.wait_ge(keys_done, T.add("keys"))
                for h in range(2):
                    take(tile(mid_hi[:, KN:], h), bank[3 + h][:, :])
                act.wait_ge(chunk_done[1], T.now("slot1"))
                for h in range(2):
                    take(tile(mid_hi[:, VV:], h), bank[5 + h][:, :])
                exps(0)
                split(1)
                exps(1)
                for h in range(2):
                    for qi in range(TOK):
                        act.wait_ge(probs_turned, T.add("turned"))
                        take(turned_view(mid_hi, h, qi), turned_bank(qi))

            def stream(rounds, sizes, **drains):
                per = len(sizes)
                with T.loop(act, rounds, slot0=per // 2, slot1=per // 2, **drains):
                    for c, n in enumerate(sizes):
                        split(c % 2, n)
                    T.add("b1", drains.get("b1", 0))

            def silus():
                act.wait_ge(drained[1], T.add("b1"))
                for b in range(2):
                    act.activation(tile(work, 2 + b), tile(work, b), ACT.Silu).then_inc(silu_done, 1)

            def ffn(last):
                split(0)
                rms(4, D)
                silus()
                split(1)
                with T.loop(act, KF // 2 - 1, slot0=1, slot1=1, b1=1):
                    split(0)
                    silus()
                    split(1)
                if last:
                    for c in range(10):
                        split(c % 2, DOWN_AHEAD[c % 6])
                else:
                    stream(2, DOWN_AHEAD)

            stream(2, [SLOT] * 2, b1=1)
            ffn(False)
            for c in range(12):
                split(c % 2)
                if c == 0:
                    rms(6, D)
            T.add("b1", 4)
            stream(2, [SLOT] * 2, b1=1)
            ffn(True)
            rms(0, D)

        @block.vector
        def _(v):
            T = Tally()

            def do(instruction):
                instruction.then_inc(step, 1)
                T.add("step")

            def settle():
                v.wait_ge(step, T.now("step"))

            def drain(b, instruction):
                instruction.then_inc(drained[b], 1)
                T.add(f"b{b}")

            def ready(instruction):
                instruction.then_inc(operand_ready, 1)
                T.add("operand")

            def all_ready():
                v.wait_ge(operand_ready, T.now("operand"))

            def landed(*banks):
                for b in banks:
                    v.wait_ge(drained[b], T.now(f"b{b}"))

            def done(s):
                v.wait_ge(chunk_done[s], T.now(f"slot{s}"))

            def split(s, n=SLOT):
                v.wait_ge(hi_split[s], T.add(f"slot{s}"))
                v.tensor_tensor(w_lo[s][:, 0:n], raw[s][:, 0:n], w_hi[s][:, 0:n], ALU.subtract).then_inc(w_split[s], 1)

            def gain(name, m):
                return vec[:, ds(m + VEC[name], 1)] if not isinstance(m, int) else vec[:, VEC[name] + m:VEC[name] + m + 1]

            def at(t, m):
                return t[:, ds(m * SEQ, SEQ)]

            def normed(name, ms):
                for m in ms:
                    do(v.tensor_scalar(at(a_hi, m), at(xT, m), gain(name, m), None, ALU.mult))
                settle()
                for m in ms:
                    ready(v.scalar_tensor_tensor(at(a_lo, m), at(xT, m), gain(name, m), at(a_hi, m).bitcast(F32),
                                                 ALU.mult, ALU.subtract))

            def clear_acc():
                do(v.memset(acc[:, :], 0.0))
                settle()

            def squares(tiles):
                for t in tiles:
                    wait(v, squares_added, T.now("squares"))
                    do(v.tensor_tensor(sq[:, :], t, t, ALU.mult))
                    settle()
                    v.tensor_tensor(acc[:, :], acc[:, :], sq[:, :], ALU.add).then_inc(squares_added, 1)
                    T.add("squares")

            def inverse_rms(b, dst=None):
                v.wait_ge(rms_done, T.add("rms"))
                if dst is None:
                    do(v.reciprocal(bank[b][:, :], bank[b][:, :]))
                    settle()
                else:
                    drain(b, v.reciprocal(dst[:, :], bank[b][:, :]))
                    landed(b)

            def scaled(m, b):
                drain(b, v.tensor_tensor(tile(work, m), bank[b][:, :], rstd[:, :], ALU.mult))

            def lo(dst, src, hi):
                return v.tensor_tensor(dst, src, hi, ALU.subtract)

            def rotate(dst, tmp, src, b=None):
                do(v.tensor_tensor(dst, src, cos[:, :], ALU.mult))
                for g in range(4):
                    to, of = slice(HALF * g, HALF * (g + 1)), slice(HALF * (g ^ 1), HALF * ((g ^ 1) + 1))
                    part = v.tensor_tensor(tmp[to, :], src[of, :], sin[of, :], ALU.mult)
                    if g == 3 and b is not None:
                        drain(b, part)
                        landed(b)
                    else:
                        do(part)
                settle()
                do(v.tensor_tensor(dst, dst, tmp, ALU.add))
                settle()

            v.memset(eps[:, :], EPS)
            v.memset(ones[:, :], 1.0).then_inc(ones_made, 1)
            mask_q, mask_k = (mid_hi[:, c:c + P].bitcast(F32) for c in (MASK_Q, MASK_K))
            v.memset(mask_q[:, 0:P // 2], 1.0)
            v.memset(mask_q[:, P // 2:P], 0.0)
            v.memset(mask_k[:, 0:P // 2], 0.0)
            v.memset(mask_k[:, P // 2:P], MASKED).then_inc(masks_made, 1)

            v.wait_ge(positions_loaded, 16)
            do(v.tensor_copy(tile(work, 4), tile(work, 5).bitcast(I32)))
            settle()
            v.wait_ge(vectors_loaded, 16)
            do(v.tensor_scalar(tile(work, 2), tile(work, 4), vec[:, FREQ:FREQ + 1], None, ALU.mult))
            for unit in (2048.0, 1.0):
                settle()
                do(v.tensor_scalar(tile(work, 3), tile(work, 2), 1.0 / (2 * math.pi * unit), ROUND, ALU.mult, ALU.add))
                settle()
                do(v.tensor_scalar(tile(work, 3), tile(work, 3), ROUND, None, ALU.subtract))
                for part in two_pi_parts():
                    settle()
                    do(v.scalar_tensor_tensor(tile(work, 2), tile(work, 3), -part * unit, tile(work, 2), ALU.mult, ALU.add))
            settle()
            v.tensor_scalar(tile(work, 0), tile(work, 2), PI_BELOW, -PI_BELOW, ALU.min, ALU.max).then_inc(angles_ready, 1)
            v.wait_ge(angles_ready, 1)
            do(v.scalar_tensor_tensor(tile(work, 4), tile(work, 0), -1.0, tile(work, 0), ALU.mult, ALU.max))
            settle()
            v.tensor_scalar(tile(work, 1), tile(work, 4), -1.0, math.pi / 2, ALU.mult, ALU.add).then_inc(angles_ready, 1)

            for j in range(KD // 2):
                v.wait_ge(x_loaded[j], 16)
                normed("mla_norm", [2 * j, 2 * j + 1])
                if j == 0:
                    split(0)
            split(1)
            clear_acc()
            squares([tile(xT, m) for m in range(KD)])
            v.wait_ge(trig_done, 2)

            inverse_rms(7, rstd)
            done(0)
            scaled(0, 0)
            scaled(1, 1)
            split(0)
            done(1)
            scaled(2, 2)
            scaled(3, 3)
            split(1, KR_N)
            landed(0, 1, 2, 3)
            clear_acc()
            squares([tile(work, m) for m in range(KQ)])
            done(0)
            scaled(4, 4)
            scaled(5, 5)
            split(0, UQ_N)
            inverse_rms(7)

            def normalise(name, m0, tiles, b):
                for t in range(tiles):
                    ins = v.scalar_tensor_tensor(tile(work, m0 + t), tile(work, m0 + t), gain(name, t), bank[b][:, :], ALU.mult, ALU.mult)
                    if t < tiles - 1:
                        do(ins)
                    else:
                        drain(b, ins)
                settle()
                landed(b)

            def operands(m0, tiles):
                for t in range(m0, m0 + tiles):
                    do(v.tensor_copy(tile(a_hi, t), tile(work, t)))
                    settle()
                    ready(lo(tile(a_lo, t), tile(work, t), tile(a_hi, t)))

            clear_acc()
            landed(4, 5)
            squares([tile(work, KQ + m) for m in range(KKV)])
            normalise("mla_g_cq", 0, KQ, 7)
            done(1)
            operands(0, KQ)
            split(1, UKV_N)
            inverse_rms(0)
            normalise("mla_g_ckv", KQ, KKV, 0)
            operands(KQ, KKV)
            scaled(0, 6)
            landed(6)
            rotate(tile(work, 1), tile(work, 2), tile(work, 0))
            for h in range(2):
                own, other = slice(h * ROPE, (h + 1) * ROPE), slice((1 - h) * ROPE, (2 - h) * ROPE)
                hi_t, lo_t = tile(a_hi, KQ + KKV + h), tile(a_lo, KQ + KKV + h)
                do(v.memset(hi_t[other, :].bitcast(F32), 0.0))
                do(v.memset(lo_t[other, :].bitcast(F32), 0.0))
                do(v.tensor_copy(hi_t[own, :], tile(work, 1)[own, :]))
                settle()
                ins = lo(lo_t[own, :], tile(work, 1)[own, :], hi_t[own, :])
                if h == 0:
                    do(ins)
                else:
                    ready(ins)
            all_ready()

            def taken():
                v.wait_ge(hi_taken, T.add("taken"))

            def row_maxima(h):
                for qi in range(TOK):
                    k, L = h * TOK + qi, (qi + 1) * P
                    v.wait_ge(scores_done, T.add("scores"))
                    do(v.tensor_reduce(row_max[:, k:k + 1], bank[qi][:, 0:L], AX_X, ALU.max))
                    settle()
                    v.tensor_scalar(exp_bias[:, k:k + 1], row_max[:, k:k + 1], -SCALE, None, ALU.mult).then_inc(max_ready, 1)

            def normalised(h):
                for qi in range(TOK):
                    k, p0 = h * TOK + qi, PROB[h][qi]
                    v.wait_ge(drained[qi], T.add(f"b{qi}"))
                    do(v.reciprocal(row_inv[:, k:k + 1], row_sum[:, k:k + 1]))
                    settle()
                    pr = work[:, p0:p0 + (qi + 1) * P]
                    v.tensor_scalar(pr, pr, row_inv[:, k:k + 1], None, ALU.mult).then_inc(probs_ready, 1)

            with T.loop(v, PAIRS, slot0=1, slot1=1, taken=14, step=24, scores=8, heads=2,
                        b0=3, b1=3, b2=3, b3=3, b4=5, b5=5, b6=2, b7=1) as i:
                done(0)
                for h in range(2):
                    taken()
                    drain(h, lo(tile(mid_lo[:, QN:], h), bank[h][:, :], tile(mid_hi[:, QN:], h)))
                rotate(tile(work, 0), tile(work, 1), bank[2][:, :], b=2)
                do(v.tensor_copy(tile(mid_hi[:, QR:], 0), tile(work, 0)))
                settle()
                lo(tile(mid_lo[:, QR:], 0), tile(work, 0), tile(mid_hi[:, QR:], 0)).then_inc(rope_ready, 1)
                for h in range(2):
                    taken()
                    drain(3 + h, lo(tile(mid_lo[:, KN:], h), bank[3 + h][:, :], tile(mid_hi[:, KN:], h)))
                for h in range(2):
                    taken()
                    drain(5 + h, lo(tile(mid_lo[:, VV:], h), bank[5 + h][:, :], tile(mid_hi[:, VV:], h)))
                row_maxima(0)
                normalised(0)
                row_maxima(1)
                split(0)
                normalised(1)
                split(1)
                for h in range(2):
                    for qi in range(TOK):
                        taken()
                        drain(4 + qi % 2, lo(turned_view(mid_lo, h, qi), turned_bank(qi), turned_view(mid_hi, h, qi)))
                for h in range(2):
                    o = i * (2 * SEQ) + (OO + h * SEQ)
                    v.wait_ge(head_done, T.add("heads"))
                    do(v.tensor_copy(mid_hi[:, ds(o, SEQ)], bank[6 + h][:, :]))
                    settle()
                    drain(6 + h, lo(mid_lo[:, ds(o, SEQ)], bank[6 + h][:, :], mid_hi[:, ds(o, SEQ)]))

            def residual(banks, ms, name):
                for b, m in zip(banks, ms):
                    drain(b, v.tensor_tensor(at(xT, m), bank[b][:, :], at(xT, m), ALU.add))
                landed(*banks)
                if name:
                    normed(name, ms)
                squares([at(xT, m) for m in ms])

            def two_pairs(name):
                with T.loop(v, 2, slot0=1, slot1=1, b0=1, b1=1, b2=1, b3=1, step=8, squares=4, operand=4) as i:
                    for s in range(2):
                        done(s)
                        residual([2 * s, 2 * s + 1], [i * 4 + (2 * s + k) for k in range(2)], name)
                        split(s)

            def ffn_round(f, first=False):
                done(0)
                all_ready()
                if first:
                    inverse_rms(4, rstd)
                    clear_acc()
                scaled(0, 0)
                scaled(1, 1)
                split(0)
                for b in range(2):
                    v.wait_ge(silu_done, T.add("silu"))
                    do(v.tensor_tensor(tile(work, 2 + b), tile(work, 2 + b), rstd[:, :], ALU.mult))
                settle()
                all_ready()
                done(1)
                for b in range(2):
                    drain(2 + b, v.tensor_tensor(tile(work, 4 + b), bank[2 + b][:, :], tile(work, 2 + b), ALU.mult))
                landed(2, 3)
                inner_operands(f, 4)
                split(1)

            def inner_operands(f, w):
                for b in range(2):
                    do(v.tensor_copy(at(mid_hi, f + b), tile(work, w + b)))
                settle()
                for b in range(2):
                    ready(lo(at(mid_lo, f + b), tile(work, w + b), at(mid_hi, f + b)))

            def ffn(name):
                ffn_round(0, first=True)
                with T.loop(v, KF // 2 - 1, slot0=1, slot1=1, b0=1, b1=1, b2=1, b3=1, step=4, silu=2, operand=2) as i:
                    ffn_round(i * 2 + 2)

                def down_round(m, last):
                    for c in range(6):
                        if c % 3 == 2:
                            pair = c // 3
                            done(c % 2)
                            residual([4 + 2 * pair, 5 + 2 * pair], [m + (2 * pair + k) for k in range(2)], name)
                        if not (last and c >= 4):
                            split(c % 2, DOWN_AHEAD[c])
                if name:
                    with T.loop(v, 2, slot0=3, slot1=3, b4=1, b5=1, b6=1, b7=1, step=8, squares=4, operand=4) as i:
                        down_round(i * 4, False)
                else:
                    down_round(0, False)
                    down_round(4, True)

            clear_acc()
            two_pairs("ffn_norm0")
            ffn("conv_norm")

            for c in range(12):
                m, part = c // 3 * 2, c % 3
                all_ready()
                done(c % 2)
                if c == 0:
                    inverse_rms(6, rstd)
                    clear_acc()
                scaled(2 * part, 2 * part)
                scaled(2 * part + 1, 2 * part + 1)
                split(c % 2)
                if part < 2:
                    continue
                landed(0, 1, 2, 3, 4, 5)
                B, u, y = ([tile(work, w + b) for b in range(2)] for w in (0, 4, 2))
                tap = [[vec[:, VEC["conv_w"] + t * KD + m + b:VEC["conv_w"] + t * KD + m + b + 1] for b in range(2)] for t in range(CONV)]
                for b in range(2):
                    do(v.tensor_tensor(u[b], y[b], u[b], ALU.mult))
                settle()
                for b in range(2):
                    do(v.tensor_scalar(y[b], u[b], tap[CONV - 1][b], None, ALU.mult))
                for back in range(1, CONV):
                    settle()
                    for b in range(2):
                        do(v.scalar_tensor_tensor(y[b][:, back:], u[b][:, 0:SEQ - back], tap[CONV - 1 - back][b], y[b][:, back:],
                                                  ALU.mult, ALU.add))
                settle()
                for b in range(2):
                    do(v.tensor_tensor(B[b], B[b], y[b], ALU.mult))
                settle()
                inner_operands(m, 0)

            two_pairs("ffn_norm1")
            ffn(None)

            inverse_rms(0, rstd)
            wait(v, squares_added, T.now("squares"))
            for m in range(KD):
                v.scalar_tensor_tensor(tile(xT, m), tile(xT, m), gain("final_norm", m), rstd[:, :], ALU.mult, ALU.mult).then_inc(y_ready, 1)


def columns(w, cols):
    return w.reshape(-1, P, w.shape[1])[:, :, cols].transpose(1, 0, 2).reshape(P, -1)


def weight_stream(w):
    def span(c0, n=2 * P):
        return list(range(c0, c0 + n))

    w_in, uq, ukv = w["mla_w_in"][0], w["mla_w_uq"][0], w["mla_w_ukv"][0]
    yield columns(w_in, span(0))
    yield columns(w_in, span(2 * P))
    yield columns(w_in, span(QRANK))
    yield columns(w_in, span(QRANK + KVRANK, ROPE) * 2)
    for h in range(0, HEADS, 2):
        q, kv = NOPE + ROPE, NOPE + VDIM
        yield columns(uq, [c for at, n in ((0, NOPE), (NOPE, ROPE)) for g in (h, h + 1) for c in span(g * q + at, n)])
        yield columns(ukv, [c for at, n in ((0, NOPE), (NOPE, VDIM)) for g in (h, h + 1) for c in span(g * kv + at, n)])
    for m in range(KD // 2):
        yield columns(w["mla_w_o"][0], span(m * 2 * P))
    for layer in range(2):
        if layer == 1:
            for m in range(KD // 2):
                for part in range(3):
                    yield columns(w["conv_w_in"][0], span(part * D + m * 2 * P))
            for m in range(KD // 2):
                yield columns(w["conv_w_out"][0], span(m * 2 * P))
        for f in range(KF // 2):
            yield columns(w["ffn_w_gate"][layer], span(f * 2 * P))
            yield columns(w["ffn_w_up"][layer], span(f * 2 * P))
        for m in range(KD // 2):
            for ks in DOWN_K:
                yield columns(w["ffn_w_down"][layer][ks[0] * P:(ks[-1] + 1) * P], span(m * 2 * P))


def kernel(**inputs):
    import concourse.bacc as bacc
    from concourse.bass_utils import run_bass_kernel_spmd

    w = {name: np.asarray(a) for name, a in inputs.items()}
    chunks = list(weight_stream(w))
    weights = np.zeros((len(chunks), P, SLOT), np.float32)
    for c, chunk in enumerate(chunks):
        weights[c, :, :chunk.shape[1]] = chunk
    rows = [w["mla_norm"], w["mla_g_cq"], w["mla_g_ckv"], w["ffn_norm"][0:1], w["conv_norm"], w["ffn_norm"][1:2],
            w["final_norm"][None], w["conv_w"][0]]
    freq = np.float32(1) / np.power(10000.0, np.arange(0, ROPE, 2) / ROPE).astype(np.float32)
    constants = np.stack([np.tile(freq, P // HALF), np.tile(np.repeat([1, -1], HALF), P // ROPE)]).astype(np.float32)
    vectors = np.concatenate([r.reshape(-1, P) for r in rows] + [constants]).T
    arrays = {
        "xt": np.ascontiguousarray(w["x"][0].T),
        "positions": w["positions"],
        "vectors": np.ascontiguousarray(vectors),
        "weights_in": weights,
    }
    nc = bacc.Bacc("TRN2", target_bir_lowering=False, num_devices=1)
    args = {n: nc.dram_tensor(n, a.shape, mybir.dt.from_np(a.dtype), kind="ExternalInput").ap() for n, a in arrays.items()}
    out = nc.dram_tensor("out", (D, SEQ), F32, kind="ExternalOutput").ap()
    build(nc, **args, out=out)
    result = run_bass_kernel_spmd(nc, [arrays], core_ids=[0])
    return np.ascontiguousarray(result.results[0]["out"].T)[None]
```

```python
from collections import Counter
from contextlib import ExitStack, contextmanager
import math

import numpy as np

import concourse.bass as bass
from concourse import mybir

F32 = mybir.dt.float32
F32R = mybir.dt.float32r
I32 = mybir.dt.int32
ALU = mybir.AluOpType
ACT = mybir.ActivationFunctionType
AX_X = mybir.AxisListType.X
ds = bass.ds

P = 128
SEQ = 512
TOK = SEQ // P
D = 1024
KD = D // P
HEADS, NOPE, ROPE, VDIM = 8, 128, 64, 128
QRANK, KVRANK = 512, 256
KQ, KKV = QRANK // P, KVRANK // P
D_FF = (8 * D // 3 + 255) // 256 * 256
KF = D_FF // P
CONV = 3
EPS = 1e-6
SCALE = 1.0 / math.sqrt(NOPE + ROPE)
HALF = ROPE // 2
SLOT = KD * 2 * P
PAIRS = HEADS // 2
DOWN_K = [range(0, 8), range(8, 16), range(16, KF)]
UQ_N = KQ * 2 * (NOPE + ROPE)
UKV_N = KKV * 2 * (NOPE + VDIM)
KR_N = KD * 2 * ROPE
DOWN_N = [len(ks) * 2 * P for ks in DOWN_K]
DOWN_AHEAD = (DOWN_N * 3)[2:8]

VEC_ROWS = [("mla_norm", KD), ("mla_g_cq", KQ), ("mla_g_ckv", KKV), ("ffn_norm0", KD), ("conv_norm", KD),
            ("ffn_norm1", KD), ("final_norm", KD), ("conv_w", CONV * KD)]
VEC = {}
for _name, _rows in VEC_ROWS:
    VEC[_name] = sum(r for _, r in VEC_ROWS[:len(VEC)])
N_VEC = sum(r for _, r in VEC_ROWS)
FREQ, SIGN, HALF_PI, HEAD_MASK = N_VEC, N_VEC + 1, N_VEC + 2, N_VEC + 3
N_COLS = N_VEC + 5

PT_STEP = 3 * P
QN, QR = 0, 2 * SEQ
KN = QR + SEQ
VV = KN + 2 * SEQ
PT = [VV + TOK * 2 * VDIM, VV + TOK * 2 * VDIM + TOK * PT_STEP + P]
OO = PT[1] + TOK * PT_STEP + P
CKV = OO + (HEADS - KKV) * SEQ
MASK_Q = OO + HEADS * SEQ
MASK_K = MASK_Q + P
assert MASK_K + P <= KF * SEQ
PI_BELOW = 3.1415925
ROUND = 1.5 * 2.0 ** 23
MASKED = -float(2.0 ** 93)

Q_BANKS, K_BANKS, V_BANKS, TURNED, HEAD_BANKS = (4, 5, 6), (1, 2), (4, 5), (7, 0), (3, 7)
W_O_BANKS, DOWN_BANKS, CONV_OUT_BANKS = ((4, 5), (1, 2)), ((4, 5), (6, 7)), ((0, 1), (2, 3))
ROUND_USES = dict(b0=6, b1=3, b2=3, b3=3, b4=2, b5=2, b6=1, b7=5)

PROB = [[h * 1280 + x for x in (0, 128, 384, 768)] for h in range(2)]


def two_pi_parts():
    rest, parts = 2 * math.pi, []
    for _ in range(2):
        exponent = math.floor(math.log2(rest))
        unit = 2.0 ** (exponent - 11)
        parts.append(math.floor(rest / unit) * unit)
        rest -= parts[-1]
    return parts + [rest]


class Tally:

    def __init__(self):
        self.base, self.here, self.per, self.i = Counter(), Counter(), {}, None

    def add(self, name, k=1):
        self.here[name] += k
        return self.now(name)

    def now(self, name):
        n = self.base[name] + self.here[name]
        per = self.per.get(name, 0)
        return n if self.i is None or not per else self.i * per + n

    @contextmanager
    def loop(self, engine, rounds, **per):
        self.base, self.here = self.base + self.here, Counter()
        with engine.Fori(0, rounds) as i:
            self.per, self.i = per, i
            yield i
            assert dict(+self.here) == per, (dict(self.here), per)
        self.base += Counter({k: v * rounds for k, v in per.items()})
        self.here, self.per, self.i = Counter(), {}, None


def wait(engine, semaphore, count):
    if not (isinstance(count, int) and count == 0):
        engine.wait_ge(semaphore, count)


def turned_view(t, h, qi):
    c0 = PT[h] + qi * P
    return t[:, c0:c0 + TOK * PT_STEP].rearrange("p (j c) -> p j c", j=TOK)[:, 0:qi + 1, 0:P]


def build(nc, xt, positions, vectors, weights_in, out):
    with ExitStack() as ctx:
        def sb(name, cols, dt=F32):
            return ctx.enter_context(nc.sbuf_tensor(name, [P, cols], dt))

        def sem(name):
            return ctx.enter_context(nc.semaphore(name))

        xT = sb("xT", KD * SEQ)
        a_hi, a_lo = sb("a_hi", KD * SEQ, F32R), sb("a_lo", KD * SEQ, F32R)
        mid_hi, mid_lo = sb("mid_hi", KF * SEQ, F32R), sb("mid_lo", KF * SEQ, F32R)
        raw = [sb(f"raw{s}", SLOT) for s in range(2)]
        w_hi = [sb(f"w_hi{s}", SLOT, F32R) for s in range(2)]
        w_lo = [sb(f"w_lo{s}", SLOT, F32R) for s in range(2)]
        work = sb("work", 6 * SEQ)
        cos, sin = sb("cos", SEQ), sb("sin", SEQ)
        rstd = sb("rstd", SEQ)
        acc = sb("acc", SEQ)
        sq = sb("sq", SEQ)
        ident, ones = sb("ident", P), sb("ones", P)
        vec = sb("vec", N_COLS)
        row_max, exp_bias, row_sum, row_inv = (sb(n, 8) for n in ("row_max", "exp_bias", "row_sum", "row_inv"))
        token_rms = sb("token_rms", TOK)
        query_scale = sb("query_scale", TOK)
        eps = sb("eps", 1)
        bank = [ctx.enter_context(nc.psum_tensor(f"bank{b}", [P, SEQ], F32)) for b in range(8)]
        A, MID = (a_hi, a_lo), (mid_hi, mid_lo)
        LATENT = tuple(t[:, CKV:CKV + KKV * SEQ] for t in MID)
        HEAD_OUT = tuple(t[:, OO:OO + HEADS * SEQ] for t in MID)

        def tile(t, m, n=SEQ):
            return t[:, m * SEQ:m * SEQ + n]

        x_squares = [tile(work, m) for m in range(6)] + [sq[:, :], rstd[:, :]]

        def tap(t, m):
            return vec[:, VEC["conv_w"] + t * KD + m:VEC["conv_w"] + t * KD + m + 1]

        def turned_bank(qi):
            return bank[TURNED[qi % 2]][:, 0:(qi + 1) * P].rearrange("p (j c) -> p j c", c=P)

        x_loaded = [sem(f"x_loaded{j}") for j in range(KD // 2)]
        positions_loaded, vectors_loaded = sem("positions_loaded"), sem("vectors_loaded")
        raw_loaded = [sem(f"raw_loaded{s}") for s in range(2)]
        half_loaded, half_hi, half_split = sem("half_loaded"), sem("half_hi"), sem("half_split")
        hi_split = [sem(f"hi_split{s}") for s in range(2)]
        w_split = [sem(f"w_split{s}") for s in range(2)]
        chunk_done = [sem(f"chunk_done{s}") for s in range(2)]
        drained = [sem(f"drained{b}") for b in range(8)]
        operand_ready = sem("operand_ready")
        hi_taken = sem("hi_taken")
        x_squared = sem("x_squared")
        squared = sem("squared")
        taps_started = sem("taps_started")
        x_squares_added = sem("x_squares_added")
        squares_added = sem("squares_added")
        stat_summed = sem("stat_summed")
        token_scales = sem("token_scales")
        rms_spread = sem("rms_spread")
        rms_done = sem("rms_done")
        silu_done = sem("silu_done")
        angles_ready, trig_done = sem("angles_ready"), sem("trig_done")
        masks_made, ones_made, ident_made = sem("masks_made"), sem("ones_made"), sem("ident_made")
        keys_done = sem("keys_done")
        rope_ready = sem("rope_ready")
        scores_done = sem("scores_done")
        max_ready = sem("max_ready")
        rotary_done = sem("rotary_done")
        inverse_ready = sem("inverse_ready")
        probs_ready = sem("probs_ready")
        probs_turned = sem("probs_turned")
        head_done = sem("head_done")
        y_ready = sem("y_ready")
        out_stored = sem("out_stored")
        step = sem("step")
        own = sem("own")

        block = ctx.enter_context(nc.Block())

        @block.sync
        def _(sp):
            T = Tally()
            def load_x(j):
                sp.dma_start(xT[:, 2 * j * SEQ:2 * (j + 1) * SEQ].rearrange("p (t s) -> p t s", t=2),
                             xt[2 * j * P:2 * (j + 1) * P, :].rearrange("(t p) s -> p t s", p=P)).then_inc(x_loaded[j], 16)

            def load(s, c, n=SLOT):
                wait(sp, w_split[s], T.add(f"slot{s}") - 1)
                sp.dma_start(raw[s][:, 0:n].rearrange("p (o n) -> p o n", o=1),
                             weights_in[ds(c, 1), :, 0:n].rearrange("o p n -> p o n")).then_inc(raw_loaded[s], 16)

            def loads(c0, rounds, sizes):
                per = len(sizes)
                with T.loop(sp, rounds, slot0=per // 2, slot1=per // 2) as i:
                    for k, n in enumerate(sizes):
                        load(k % 2, i * per + (c0 + k), n)
                return c0 + rounds * per

            sp.dma_start(vec[:, :], vectors).then_inc(vectors_loaded, 16)
            sp.dma_start(raw[0][:, 0:SLOT // 2], weights_in[0, :, 0:SLOT // 2]).then_inc(half_loaded, 16)
            load_x(0)
            T.add("slot0")
            sp.dma_start(raw[0][:, SLOT // 2:], weights_in[0, :, SLOT // 2:]).then_inc(raw_loaded[0], 16)
            for j in range(1, KD // 2):
                load_x(j)
            for c, n in enumerate([SLOT, SLOT, SLOT, KR_N, UKV_N, UQ_N]):
                if c > 0:
                    load(c % 2, c, n)
            c = loads(6, PAIRS - 1, [UQ_N, UKV_N])
            c = loads(c, 2, [SLOT] * 2)
            for layer in range(2):
                c = loads(c, KF // 2, [SLOT] * 2)
                c = loads(c, 2, DOWN_N * 2)
                if layer == 0:
                    c = loads(c, 8, [SLOT] * 2)
            for m in range(KD):
                sp.wait_ge(y_ready, m + 1)
                sp.dma_start(out[m * P:(m + 1) * P, :], tile(xT, m)).then_inc(out_stored, 16)
            sp.wait_ge(out_stored, 16 * KD)

        @block.gpsimd
        def _(pool):
            pool.dma_start(sin[:, :].bitcast(I32), positions.partition_broadcast(P)).then_inc(positions_loaded, 16)
            n = [0]

            def do(instruction):
                instruction.then_inc(own, 1)
                n[0] += 1
                pool.wait_ge(own, n[0])

            pool.wait_ge(x_squared, 2)
            do(pool.tensor_tensor(acc[:, :], x_squares[0], x_squares[1], ALU.add))
            for m in range(2, KD - 1):
                pool.wait_ge(x_squared, m + 1)
                do(pool.tensor_tensor(acc[:, :], acc[:, :], x_squares[m], ALU.add))
            pool.wait_ge(x_squared, KD)
            pool.tensor_tensor(acc[:, :], acc[:, :], x_squares[KD - 1], ALU.add).then_inc(x_squares_added, 1)

            do(pool.memset(ident[:, :], 0.0))
            pool.affine_select(out=ident[:, :], in_=ident[:, :], compare_op=ALU.not_equal, fill=1.0, base=0,
                               pattern=[[-1, P]], channel_multiplier=1).then_inc(ident_made, 1)

        @block.tensor
        def _(pe):
            T = Tally()

            def open_bank(b):
                wait(pe, drained[b], T.add(f"b{b}") - 1)

            def taken(b):
                pe.wait_ge(drained[b], T.now(f"b{b}"))

            def product(o, lhs, rhs, start, stop):
                pe.matmul(o, lhs[0], rhs[0], start=start, stop=False, skip_group_check=True)
                pe.matmul(o, lhs[0], rhs[1], start=False, stop=False, skip_group_check=True)
                return pe.matmul(o, lhs[1], rhs[0], start=False, stop=stop, skip_group_check=True)

            def slot(s, c0):
                return w_hi[s][:, c0:c0 + P], w_lo[s][:, c0:c0 + P]

            def operand(buf, k):
                return tile(buf[0], k), tile(buf[1], k)

            def chunk(s, banks, buf, ks=range(KD), first=True, last=True, ready=None, n0=0):
                pe.wait_ge(w_split[s], T.add(f"slot{s}"))
                if first:
                    for b in banks:
                        open_bank(b)
                k_tiles(s, banks, buf, ks, first, last, ready, n0).then_inc(chunk_done[s], 1)

            def k_tiles(s, banks, buf, ks, first, last, ready=None, n0=0):
                for n, k in enumerate(ks):
                    if ready is not None:
                        pe.wait_ge(operand_ready, ready + k + 1)
                    for m, b in enumerate(banks):
                        mm = product(bank[b][:, :], slot(s, ((n0 + n) * len(banks) + m) * P), operand(buf, k),
                                     first and n == 0, last and n == len(ks) - 1)
                return mm

            def stat(b, tiles):
                if tiles:
                    pe.wait_ge(squares_added, T.add("squares", tiles))
                open_bank(b)
                pe.matmul(bank[b][:, :], ones[:, :], acc[:, :], start=True, stop=True).then_inc(stat_summed, 1)

            def token_stat(b, tiles):
                pe.wait_ge(squares_added, T.add("squares", tiles))
                open_bank(b)
                for j in range(TOK):
                    mm = pe.matmul(bank[b][:, j:j + 1], acc[:, j * P:(j + 1) * P], ones[:, 0:1], start=True, stop=True)
                mm.then_inc(stat_summed, 1)

            pe.wait_ge(ones_made, 1)
            pe.wait_ge(half_split, 1)
            k_tiles(0, [0, 1], A, range(KD // 2), True, False, 0)
            chunk(0, [0, 1], A, range(KD // 2, KD), False, True, 0, n0=KD // 2)
            T.add("b0")
            T.add("b1")
            pe.wait_ge(x_squares_added, 1)
            stat(7, 0)
            chunk(1, [2, 3], A)
            stat(6, KKV)
            chunk(0, [4, 5], A)
            chunk(1, [0], A)
            made = KD

            def key(s, h):
                b = K_BANKS[h]
                open_bank(b)
                for k in range(KKV):
                    mm = product(bank[b][:, :], slot(s, (k * 4 + h) * P), operand(LATENT, k), k == 0, k == KKV - 1)
                if h == 1:
                    mm.then_inc(keys_done, 1)

            def query(s, m, ready=None):
                b = Q_BANKS[m]
                open_bank(b)
                for k in range(KQ):
                    if ready is not None:
                        pe.wait_ge(operand_ready, ready + k + 1)
                    mm = product(bank[b][:, :], slot(s, (k * 3 + m) * P), operand(A, k), k == 0, k == KQ - 1)
                if m == 2:
                    mm.then_inc(rotary_done, 1)
                if m == 1:
                    mm.then_inc(chunk_done[s], 1)

            def values(s):
                for j in range(TOK):
                    b = V_BANKS[j // 2]
                    if j % 2 == 0:
                        open_bank(b)
                    for k in range(KKV):
                        c = tuple(t[:, k * SEQ + j * P:k * SEQ + (j + 1) * P] for t in LATENT)
                        wv = tuple(t[:, (k * 4 + 2) * P:(k * 4 + 4) * P] for t in (w_hi[s], w_lo[s]))
                        mm = product(bank[b][:, j % 2 * 2 * VDIM:(j % 2 + 1) * 2 * VDIM], c, wv, k == 0, k == KKV - 1)
                mm.then_inc(chunk_done[s], 1)

            def scores():
                queries = [T.now("b4") - 1, T.now("b5") - 1]
                pe.wait_ge(rope_ready, T.add("rope"))
                for h in range(2):
                    pe.wait_ge(drained[Q_BANKS[h]], queries[h])
                    if h == 0:
                        taken(K_BANKS[0])
                        taken(K_BANKS[1])
                    for qi in range(TOK):
                        L = (qi + 1) * P
                        open_bank(qi)
                        o = bank[qi][:, 0:L]
                        qn = tuple(t[:, QN + h * SEQ + qi * P:QN + h * SEQ + (qi + 1) * P] for t in MID)
                        qr = tuple(t[:, QR + qi * P:QR + (qi + 1) * P] for t in MID)
                        product(o, qn, tuple(t[:, KN + h * SEQ:KN + h * SEQ + L] for t in MID), True, False)
                        product(o, qr, tuple(tile(t, KQ + KKV + h, L) for t in A), False, False)
                        pe.matmul(bank[qi][:, L - P:L], mid_hi[:, MASK_Q:MASK_Q + P], mid_hi[:, MASK_K:MASK_K + P],
                                  start=False, stop=True, skip_group_check=True).then_inc(scores_done, 1)

            def turn(h, tiles):
                for qi in tiles:
                    pe.wait_ge(probs_ready, T.add("probs"))
                    b = TURNED[qi % 2]
                    open_bank(b)
                    for j in range(qi + 1):
                        p0 = PROB[h][qi] + j * P
                        tr = pe.transpose(bank[b][:, j * P:(j + 1) * P], work[:, p0:p0 + P], ident[:, :])
                    tr.then_inc(probs_turned, 1)
                return [(b, T.now(f"b{b}")) for b in TURNED]

            def heads(turned, values_taken):
                for b, n in values_taken:
                    pe.wait_ge(drained[b], n)
                for h, o in enumerate(HEAD_BANKS):
                    for b, n in turned[h]:
                        pe.wait_ge(drained[b], n)
                    open_bank(o)
                    for j in range(TOK):
                        v0, p0, n = VV + (j * 2 + h) * VDIM, PT[h] + j * SEQ, SEQ - j * P
                        mm = product(bank[o][:, j * P:], tuple(t[:, v0:v0 + VDIM] for t in MID),
                                     tuple(t[:, p0:p0 + n] for t in MID), j == 0, j == TOK - 1)
                    mm.then_inc(head_done, 1)

            pe.wait_ge(w_split[0], T.add("slot0"))
            pe.wait_ge(operand_ready, made + KKV)
            made += KKV
            key(0, 0)
            key(0, 1)
            token_stat(6, KQ)
            values(0)
            pe.wait_ge(w_split[1], T.add("slot1"))
            query(1, 2, ready=made)
            query(1, 0)
            query(1, 1)
            pe.wait_ge(operand_ready, made + KQ + 1)
            made += KQ + 1
            pe.wait_ge(masks_made, 1)
            pe.wait_ge(ident_made, 1)
            taken(4)
            taken(5)

            with T.loop(pe, PAIRS - 1, slot0=1, slot1=1, rope=1, probs=8, **ROUND_USES):
                values_taken = [(b, T.now(f"b{b}")) for b in V_BANKS]
                scores()
                pe.wait_ge(w_split[0], T.add("slot0"))
                query(0, 2)
                turn(0, (0, 1))
                query(0, 0)
                turned0 = turn(0, (2, 3))
                query(0, 1)
                turn(1, (0, 1))
                pe.wait_ge(w_split[1], T.add("slot1"))
                key(1, 0)
                turned1 = turn(1, (2, 3))
                key(1, 1)
                heads((turned0, turned1), values_taken)
                values(1)
            values_taken = [(b, T.now(f"b{b}")) for b in V_BANKS]
            scores()

            def output(s, m, ks):
                b = W_O_BANKS[s][m]
                if ks[0] == 0:
                    open_bank(b)
                for k in ks:
                    mm = product(bank[b][:, :], slot(s, (k * 2 + m) * P), operand(HEAD_OUT, k), k == 0, k == HEADS - 1)
                return mm

            early, half = range(HEADS - 2), (HEADS - 2) // 2
            pe.wait_ge(w_split[0], T.add("slot0"))
            output(0, 0, early)
            turn(0, (0, 1))
            output(0, 1, early)
            turned0 = turn(0, (2, 3))
            pe.wait_ge(w_split[1], T.add("slot1"))
            output(1, 0, early[:half])
            turn(1, (0, 1))
            output(1, 0, early[half:])
            turned1 = turn(1, (2, 3))
            output(1, 1, early[:half])
            heads((turned0, turned1), values_taken)
            output(1, 1, early[half:])
            for b in HEAD_BANKS:
                taken(b)
            for s in range(2):
                output(s, 0, range(HEADS - 2, HEADS))
                output(s, 1, range(HEADS - 2, HEADS)).then_inc(chunk_done[s], 1)
            for s in range(2):
                chunk(s, W_O_BANKS[s], HEAD_OUT)

            def two_pairs(buf, ready=None):
                with T.loop(pe, 2, slot0=1, slot1=1, b0=1, b1=1, b2=1, b3=1):
                    chunk(0, [0, 1], buf, ready=ready)
                    chunk(1, [2, 3], buf)

            def ffn(made):
                chunk(0, [0, 1], A, ready=made)
                stat(4, KD)
                chunk(1, [2, 3], A)
                with T.loop(pe, KF // 2 - 1, slot0=1, slot1=1, b0=1, b1=1, b2=1, b3=1):
                    chunk(0, [0, 1], A)
                    chunk(1, [2, 3], A)
                made += KD
                with T.loop(pe, 2, slot0=3, slot1=3, b4=1, b5=1, b6=1, b7=1):
                    for c in range(6):
                        pair = c // 3
                        chunk(c % 2, [4 + 2 * pair, 5 + 2 * pair], MID, DOWN_K[c % 3], c % 3 == 0, c % 3 == 2,
                              ready=made if pair == 0 else None)
                return made + KF

            made = ffn(made)
            for c in range(12):
                chunk(c % 2, [2 * (c % 3), 2 * (c % 3) + 1], A, ready=made if c == 0 else None)
                if c == 0:
                    stat(6, KD)
            made += KD
            two_pairs(MID, made)
            made += KD
            made = ffn(made)
            token_stat(0, KD)
            pe.wait_ge(token_scales, 1)
            open_bank(1)
            pe.matmul(bank[1][:, :], ones[:, :], work[:, 0:SEQ], start=True, stop=True).then_inc(rms_spread, 1)

        @block.scalar
        def _(act):
            T = Tally()

            def split(s, n=SLOT):
                k = T.add(f"slot{s}")
                act.wait_ge(raw_loaded[s], k * 16)
                wait(act, chunk_done[s], k - 1)
                act.activation(w_hi[s][:, 0:n], raw[s][:, 0:n], ACT.Copy).then_inc(hi_split[s], 1)

            def rms(b, width):
                act.wait_ge(stat_summed, T.add("stat"))
                act.activation(bank[b][:, :], bank[b][:, :], ACT.Sqrt, bias=eps[:, 0:1], scale=1.0 / width).then_inc(rms_done, 1)

            def token_rms_of(b, width):
                act.wait_ge(stat_summed, T.add("stat"))
                act.activation(token_rms[:, :], bank[b][:, 0:TOK], ACT.Sqrt, bias=eps[:, 0:1], scale=1.0 / width).then_inc(drained[b], 1)

            def take(dst, src):
                act.activation(dst, src, ACT.Copy).then_inc(hi_taken, 1)

            def square(src, dst, ring):
                wait(act, squares_added, max(0, T.add("squares") - ring))
                act.activation(dst, src, ACT.Square).then_inc(squared, 1)

            def banks_used(uses):
                for b, n in uses.items():
                    T.add(b, n)

            def square_drained(b, src, dst, ring):
                act.wait_ge(drained[b], T.add(f"b{b}"))
                square(src, dst, ring)

            def square_x(j):
                act.wait_ge(x_loaded[j], 16)
                for m in (2 * j, 2 * j + 1):
                    act.activation(x_squares[m], tile(xT, m), ACT.Square).then_inc(x_squared, 1)

            act.wait_ge(half_loaded, 16)
            act.activation(w_hi[0][:, 0:SLOT // 2], raw[0][:, 0:SLOT // 2], ACT.Copy).then_inc(half_hi, 1)
            square_x(0)
            T.add("slot0")
            act.wait_ge(raw_loaded[0], 16)
            act.activation(w_hi[0][:, SLOT // 2:], raw[0][:, SLOT // 2:], ACT.Copy).then_inc(hi_split[0], 1)
            for j in range(1, KD // 2):
                square_x(j)
            split(1)
            act.wait_ge(ones_made, 1)
            rms(7, D)
            split(0)
            for b in range(2):
                square_drained(b, tile(work, KQ + b), sq[:, :], 1)
            split(1, KR_N)
            rms(6, KVRANK)
            for m in range(KQ):
                square_drained(2 + m, tile(work, m), sq[:, :], 1)
                if m == 1:
                    split(0, UKV_N)
            split(1, UQ_N)
            banks_used(dict(b0=1, b6=1, b7=1))
            act.wait_ge(vectors_loaded, 16)
            act.wait_ge(angles_ready, 1)
            act.activation(sin[:, :], cos[:, :], ACT.Sin, scale=vec[:, SIGN:SIGN + 1]).then_inc(trig_done, 1)
            act.activation(cos[:, :], cos[:, :], ACT.Abs).then_inc(trig_done, 1)
            act.wait_ge(trig_done, 2)
            act.activation(cos[:, :], cos[:, :], ACT.Sin, bias=vec[:, HALF_PI:HALF_PI + 1], scale=-1.0).then_inc(trig_done, 1)

            def keys():
                act.wait_ge(keys_done, T.add("keys"))
                for h, b in enumerate(K_BANKS):
                    take(tile(mid_hi[:, KN:], h), bank[b][:, :])

            def queries(s):
                act.wait_ge(chunk_done[s], T.now(f"slot{s}"))
                for h in range(2):
                    take(tile(mid_hi[:, QN:], h), bank[Q_BANKS[h]][:, :])

            def values(s):
                act.wait_ge(chunk_done[s], T.now(f"slot{s}"))
                for h, b in enumerate(V_BANKS):
                    take(tile(mid_hi[:, VV:], h), bank[b][:, :])

            def exps(h):
                for qi in range(TOK):
                    act.wait_ge(max_ready, T.add("max"))
                    k, L = h * TOK + qi, (qi + 1) * P
                    act.activation(work[:, PROB[h][qi]:PROB[h][qi] + L], bank[qi][:, 0:L], ACT.Exp, bias=exp_bias[:, k:k + 1],
                                   scale=query_scale[:, qi:qi + 1], accum_out=row_sum[:, k:k + 1]).then_inc(drained[qi], 1)

            def normalised(h):
                for qi in range(TOK):
                    act.wait_ge(inverse_ready, T.add("inverse"))
                    k, pr = h * TOK + qi, work[:, PROB[h][qi]:PROB[h][qi] + (qi + 1) * P]
                    act.activation(pr, pr, ACT.Copy, scale=row_inv[:, k:k + 1]).then_inc(probs_ready, 1)

            def turned(h, tiles):
                for qi in tiles:
                    act.wait_ge(probs_turned, T.add("turned"))
                    take(turned_view(mid_hi, h, qi), turned_bank(qi))

            keys()
            token_rms_of(6, QRANK)
            values(0)
            queries(1)
            split(0, UQ_N)
            banks_used(dict(b1=1, b2=1, b4=2, b5=2, b6=2))
            with T.loop(act, PAIRS - 1, slot0=1, slot1=1, keys=1, max=8, inverse=8, turned=8, **ROUND_USES):
                exps(0)
                normalised(0)
                exps(1)
                normalised(1)
                turned(0, (0, 1))
                split(1, UKV_N)
                turned(0, (2, 3))
                queries(0)
                turned(1, (0, 1))
                turned(1, (2, 3))
                keys()
                split(0)
                values(1)
                banks_used(ROUND_USES)
            exps(0)
            normalised(0)
            exps(1)
            normalised(1)
            turned(0, (0, 1))
            split(1)
            turned(0, (2, 3))
            turned(1, range(TOK))
            banks_used(dict(b0=6, b1=2, b2=2, b3=3, b7=5))

            def residuals(banks, per, sizes, last=False):
                chunks = KD // 2 * per
                for c in range(chunks):
                    pair = c // per
                    if c % per == per - 1:
                        for h, b in enumerate(banks[pair % len(banks)]):
                            square_drained(b, tile(xT, 2 * pair + h), tile(work, 4 + h), 2)
                    if not last or c < chunks - 2:
                        split(c % 2, sizes[c % len(sizes)])

            def silus():
                act.wait_ge(drained[1], T.add("b1"))
                for b in range(2):
                    act.activation(tile(work, 2 + b), tile(work, b), ACT.Silu).then_inc(silu_done, 1)

            def ffn(last):
                split(0)
                rms(4, D)
                silus()
                split(1)
                with T.loop(act, KF // 2 - 1, slot0=1, slot1=1, b1=1):
                    split(0)
                    silus()
                    split(1)
                banks_used(dict(b0=KF // 2, b2=KF // 2, b3=KF // 2, b4=1))
                residuals(DOWN_BANKS, 3, DOWN_AHEAD, last)

            residuals(W_O_BANKS, 1, [SLOT])
            ffn(False)
            for c in range(12):
                if c % 3 == 2:
                    for b in range(2):
                        act.wait_ge(drained[4 + b], T.add(f"b{4 + b}"))
                        act.activation(tile(work, 2 + b), tile(work, 4 + b), ACT.Copy,
                                       scale=tap(CONV - 1, c // 3 * 2 + b)).then_inc(taps_started, 1)
                split(c % 2)
                if c == 0:
                    rms(6, D)
            banks_used(dict(b0=4, b1=4, b2=4, b3=4, b6=1))
            residuals(CONV_OUT_BANKS, 1, [SLOT])
            ffn(True)
            token_rms_of(0, D)

        @block.vector
        def _(v):
            T = Tally()

            def do(instruction):
                instruction.then_inc(step, 1)
                T.add("step")

            def settle():
                v.wait_ge(step, T.now("step"))

            def drain(b, instruction):
                instruction.then_inc(drained[b], 1)
                T.add(f"b{b}")

            def ready(instruction):
                instruction.then_inc(operand_ready, 1)
                T.add("operand")

            def all_ready():
                v.wait_ge(operand_ready, T.now("operand"))

            def landed(*banks):
                for b in banks:
                    v.wait_ge(drained[b], T.now(f"b{b}"))

            def done(s):
                v.wait_ge(chunk_done[s], T.now(f"slot{s}"))

            def split(s, n=SLOT):
                v.wait_ge(hi_split[s], T.add(f"slot{s}"))
                v.tensor_tensor(w_lo[s][:, 0:n], raw[s][:, 0:n], w_hi[s][:, 0:n], ALU.subtract).then_inc(w_split[s], 1)

            def gain(name, m):
                return vec[:, ds(m + VEC[name], 1)] if not isinstance(m, int) else vec[:, VEC[name] + m:VEC[name] + m + 1]

            def at(t, m):
                return t[:, ds(m * SEQ, SEQ)]

            def normed(name, ms):
                for m in ms:
                    do(v.tensor_scalar(at(a_hi, m), at(xT, m), gain(name, m), None, ALU.mult))
                settle()
                for m in ms:
                    ready(v.scalar_tensor_tensor(at(a_lo, m), at(xT, m), gain(name, m), at(a_hi, m).bitcast(F32),
                                                 ALU.mult, ALU.subtract))

            def clear_acc():
                wait(v, squares_added, T.now("squares"))
                do(v.memset(acc[:, :], 0.0))
                settle()

            def add_squares(buffers):
                for buf in buffers:
                    wait(v, squares_added, T.now("squares"))
                    v.wait_ge(squared, T.add("squares"))
                    v.tensor_tensor(acc[:, :], acc[:, :], buf, ALU.add).then_inc(squares_added, 1)

            def inverse_rms(b, dst=None):
                v.wait_ge(rms_done, T.add("rms"))
                if dst is None:
                    do(v.reciprocal(bank[b][:, :], bank[b][:, :]))
                    settle()
                else:
                    drain(b, v.reciprocal(dst[:, :], bank[b][:, :]))
                    landed(b)

            def scaled(m, b):
                drain(b, v.tensor_tensor(tile(work, m), bank[b][:, :], rstd[:, :], ALU.mult))

            def lo(dst, src, hi):
                return v.tensor_tensor(dst, src, hi, ALU.subtract)

            def rotate(dst, tmp, src, b=None):
                do(v.tensor_tensor(dst, src, cos[:, :], ALU.mult))
                for to, of in ((slice(0, ROPE), slice(ROPE, P)), (slice(ROPE, P), slice(0, ROPE))):
                    part = v.tensor_tensor(tmp[to, :], src[of, :], sin[of, :], ALU.mult)
                    if to.start and b is not None:
                        drain(b, part)
                        landed(b)
                    else:
                        do(part)
                settle()
                do(v.tensor_tensor(dst, dst, tmp, ALU.add))
                settle()

            v.memset(eps[:, :], EPS)
            v.memset(ones[:, :], 1.0).then_inc(ones_made, 1)
            mask_q, mask_k = (mid_hi[:, c:c + P].bitcast(F32) for c in (MASK_Q, MASK_K))
            v.memset(mask_q[:, 0:P // 2], 1.0)
            v.memset(mask_q[:, P // 2:P], 0.0)
            v.memset(mask_k[:, 0:P // 2], 0.0)
            v.memset(mask_k[:, P // 2:P], MASKED).then_inc(masks_made, 1)

            v.wait_ge(vectors_loaded, 16)
            for j in range(KD // 2):
                if j == 0:
                    v.wait_ge(half_hi, 1)
                    v.tensor_tensor(w_lo[0][:, 0:SLOT // 2], raw[0][:, 0:SLOT // 2], w_hi[0][:, 0:SLOT // 2], ALU.subtract).then_inc(half_split, 1)
                v.wait_ge(x_loaded[j], 16)
                normed("mla_norm", [2 * j, 2 * j + 1])
                if j == 1:
                    v.wait_ge(hi_split[0], T.add("slot0"))
                    v.tensor_tensor(w_lo[0][:, SLOT // 2:], raw[0][:, SLOT // 2:], w_hi[0][:, SLOT // 2:], ALU.subtract).then_inc(w_split[0], 1)
            split(1)

            angle, turns = cos[:, :], sin[:, :]
            v.wait_ge(positions_loaded, 16)
            do(v.tensor_copy(angle, turns.bitcast(I32)))
            settle()
            do(v.tensor_scalar(angle, angle, vec[:, FREQ:FREQ + 1], None, ALU.mult))
            settle()
            for unit in (2048.0, 1.0):
                do(v.tensor_scalar(turns, angle, 1.0 / (2 * math.pi * unit), ROUND, ALU.mult, ALU.add))
                settle()
                do(v.tensor_scalar(turns, turns, ROUND, None, ALU.subtract))
                settle()
                for part in two_pi_parts():
                    do(v.scalar_tensor_tensor(angle, turns, -part * unit, angle, ALU.mult, ALU.add))
                    settle()
            v.tensor_scalar(angle, angle, PI_BELOW, -PI_BELOW, ALU.min, ALU.max).then_inc(angles_ready, 1)

            inverse_rms(7, rstd)
            done(0)
            scaled(4, 0)
            scaled(5, 1)
            clear_acc()
            add_squares([sq[:, :]] * KKV)
            split(0)
            done(1)
            scaled(0, 2)
            scaled(1, 3)
            inverse_rms(6)
            for t in range(KKV):
                c = tile(work, KQ + t)
                ins = v.scalar_tensor_tensor(c, c, gain("mla_g_ckv", t), bank[6][:, :], ALU.mult, ALU.mult)
                if t == 0:
                    do(ins)
                else:
                    drain(6, ins)
            settle()
            landed(6)
            clear_acc()
            add_squares([sq[:, :]] * 2)
            split(1, KR_N)
            for t in range(KKV):
                do(v.tensor_copy(tile(LATENT[0], t), tile(work, KQ + t)))
            settle()
            for t in range(KKV):
                ready(lo(tile(LATENT[1], t), tile(work, KQ + t), tile(LATENT[0], t)))
            done(0)
            scaled(2, 4)
            scaled(3, 5)
            add_squares([sq[:, :]] * 2)
            split(0, UKV_N)
            done(1)
            split(1, UQ_N)
            for t in range(KQ):
                do(v.tensor_scalar(tile(a_hi, t), tile(work, t), gain("mla_g_cq", t), None, ALU.mult))
                settle()
                ready(v.scalar_tensor_tensor(tile(a_lo, t), tile(work, t), gain("mla_g_cq", t), tile(a_hi, t).bitcast(F32),
                                             ALU.mult, ALU.subtract))

            def taken():
                v.wait_ge(hi_taken, T.add("taken"))

            def keys():
                for h, b in enumerate(K_BANKS):
                    taken()
                    drain(b, lo(tile(mid_lo[:, KN:], h), bank[b][:, :], tile(mid_hi[:, KN:], h)))

            def queries():
                for h in range(2):
                    b = Q_BANKS[h]
                    taken()
                    drain(b, lo(tile(mid_lo[:, QN:], h), bank[b][:, :], tile(mid_hi[:, QN:], h)))

            def rotary_queries():
                dst = tile(work, 5)
                v.wait_ge(rotary_done, T.now("rope") + 1)
                rotate(dst, sq[:, :], bank[Q_BANKS[2]][:, :], b=Q_BANKS[2])
                do(v.tensor_copy(tile(mid_hi[:, QR:], 0), dst))
                settle()
                lo(tile(mid_lo[:, QR:], 0), dst, tile(mid_hi[:, QR:], 0)).then_inc(rope_ready, 1)
                T.add("rope")

            def values():
                for h, b in enumerate(V_BANKS):
                    taken()
                    drain(b, lo(tile(mid_lo[:, VV:], h), bank[b][:, :], tile(mid_hi[:, VV:], h)))

            def row_maxima(h):
                for qi in range(TOK):
                    k, L = h * TOK + qi, (qi + 1) * P
                    v.wait_ge(scores_done, T.add("scores"))
                    do(v.tensor_reduce(row_max[:, k:k + 1], bank[qi][:, 0:L], AX_X, ALU.max))
                    settle()
                    v.tensor_scalar(exp_bias[:, k:k + 1], row_max[:, k:k + 1], query_scale[:, qi:qi + 1], -1.0,
                                    ALU.mult, ALU.mult).then_inc(max_ready, 1)

            def inverse_sums(h):
                for qi in range(TOK):
                    k = h * TOK + qi
                    v.wait_ge(drained[qi], T.add(f"b{qi}"))
                    v.reciprocal(row_inv[:, k:k + 1], row_sum[:, k:k + 1]).then_inc(inverse_ready, 1)

            def turned(h, tiles):
                for qi in tiles:
                    taken()
                    drain(TURNED[qi % 2], lo(turned_view(mid_lo, h, qi), turned_bank(qi), turned_view(mid_hi, h, qi)))

            def heads(o):
                for h, b in enumerate(HEAD_BANKS):
                    v.wait_ge(head_done, T.add("heads"))
                    do(v.tensor_copy(HEAD_OUT[0][:, ds(o + h * SEQ, SEQ)], bank[b][:, :]))
                settle()
                for h, b in enumerate(HEAD_BANKS):
                    hi_t, lo_t = (t[:, ds(o + h * SEQ, SEQ)] for t in HEAD_OUT)
                    drain(b, lo(lo_t, bank[b][:, :], hi_t))

            keys()
            values()
            all_ready()
            scaled(0, 0)
            landed(0)
            v.wait_ge(trig_done, 3)
            rotate(tile(work, 1), tile(work, 2), tile(work, 0))
            for h in range(2):
                own_dims = vec[:, HEAD_MASK + h:HEAD_MASK + h + 1]
                do(v.tensor_scalar(tile(a_hi, KQ + KKV + h), tile(work, 1), own_dims, None, ALU.mult))
            settle()
            for h in range(2):
                own_dims = vec[:, HEAD_MASK + h:HEAD_MASK + h + 1]
                ins = v.scalar_tensor_tensor(tile(a_lo, KQ + KKV + h), tile(work, 1), own_dims,
                                             tile(a_hi, KQ + KKV + h).bitcast(F32), ALU.mult, ALU.subtract)
                if h == 0:
                    do(ins)
                else:
                    ready(ins)
            all_ready()
            v.wait_ge(drained[6], T.add("b6"))
            do(v.reciprocal(query_scale[:, :], token_rms[:, :]))
            settle()
            do(v.tensor_scalar(query_scale[:, :], query_scale[:, :], SCALE, None, ALU.mult))
            rotary_queries()
            queries()
            split(0, UQ_N)

            with T.loop(v, PAIRS - 1, slot0=1, slot1=1, taken=14, step=14, scores=8, heads=2, rope=1, **ROUND_USES) as i:
                row_maxima(0)
                inverse_sums(0)
                row_maxima(1)
                inverse_sums(1)
                turned(0, (0, 1))
                split(1, UKV_N)
                turned(0, (2, 3))
                v.wait_ge(rope_ready, T.now("rope"))
                rotary_queries()
                queries()
                turned(1, range(TOK))
                keys()
                split(0)
                heads(i * (2 * SEQ))
                values()
            row_maxima(0)
            inverse_sums(0)
            row_maxima(1)
            inverse_sums(1)
            turned(0, (0, 1))
            split(1)
            turned(0, (2, 3))
            turned(1, range(TOK))
            heads((HEADS - 2) * SEQ)

            def residual(banks, ms, name):
                for b, m in zip(banks, ms):
                    drain(b, v.tensor_tensor(at(xT, m), bank[b][:, :], at(xT, m), ALU.add))
                landed(*banks)
                if name:
                    normed(name, ms)
                add_squares([tile(work, 4), tile(work, 5)])

            def two_pairs(name):
                with T.loop(v, 2, slot0=1, slot1=1, b0=1, b1=1, b2=1, b3=1, step=4, squares=4, operand=4) as i:
                    for s in range(2):
                        done(s)
                        residual([2 * s, 2 * s + 1], [i * 4 + (2 * s + k) for k in range(2)], name)
                        split(s)

            def ffn_round(f, first=False):
                done(0)
                all_ready()
                if first:
                    inverse_rms(4, rstd)
                    clear_acc()
                scaled(0, 0)
                scaled(1, 1)
                split(0)
                for b in range(2):
                    v.wait_ge(silu_done, T.add("silu"))
                    do(v.tensor_tensor(tile(work, 2 + b), tile(work, 2 + b), rstd[:, :], ALU.mult))
                settle()
                all_ready()
                done(1)
                for b in range(2):
                    drain(2 + b, v.tensor_tensor(tile(work, 4 + b), bank[2 + b][:, :], tile(work, 2 + b), ALU.mult))
                landed(2, 3)
                inner_operands(f, 4)
                split(1)

            def inner_operands(f, w):
                for b in range(2):
                    do(v.tensor_copy(at(mid_hi, f + b), tile(work, w + b)))
                settle()
                for b in range(2):
                    ready(lo(at(mid_lo, f + b), tile(work, w + b), at(mid_hi, f + b)))

            def ffn(name):
                ffn_round(0, first=True)
                with T.loop(v, KF // 2 - 1, slot0=1, slot1=1, b0=1, b1=1, b2=1, b3=1, step=4, silu=2, operand=2) as i:
                    ffn_round(i * 2 + 2)

                def down_round(m, last):
                    for c in range(6):
                        if c % 3 == 2:
                            pair = c // 3
                            done(c % 2)
                            residual([4 + 2 * pair, 5 + 2 * pair], [m + (2 * pair + k) for k in range(2)], name)
                        if not (last and c >= 4):
                            split(c % 2, DOWN_AHEAD[c])
                if name:
                    with T.loop(v, 2, slot0=3, slot1=3, b4=1, b5=1, b6=1, b7=1, step=4, squares=4, operand=4) as i:
                        down_round(i * 4, False)
                else:
                    down_round(0, False)
                    down_round(4, True)

            clear_acc()
            for c in range(4):
                done(c % 2)
                residual(W_O_BANKS[c % 2], [2 * c, 2 * c + 1], "ffn_norm0")
                split(c % 2)
            ffn("conv_norm")

            for c in range(12):
                m, part = c // 3 * 2, c % 3
                all_ready()
                done(c % 2)
                if c == 0:
                    inverse_rms(6, rstd)
                    clear_acc()
                B, y, u = ([tile(work, w + b) for b in range(2)] for w in (0, 2, 4))
                if part < 2:
                    scaled(2 * part, 2 * part)
                    scaled(2 * part + 1, 2 * part + 1)
                    split(c % 2)
                if part == 1:
                    landed(2, 3)
                    for b in range(2):
                        do(v.tensor_tensor(y[b], y[b], rstd[:, :], ALU.mult))
                    settle()
                if part < 2:
                    continue
                for b in range(2):
                    drain(4 + b, v.tensor_tensor(u[b], bank[4 + b][:, :], y[b], ALU.mult))
                landed(0, 1, 4, 5)
                for b in range(2):
                    v.wait_ge(taps_started, m + b + 1)
                    do(v.scalar_tensor_tensor(y[b][:, 1:], u[b][:, 0:SEQ - 1], tap(CONV - 2, m + b), y[b][:, 1:], ALU.mult, ALU.add))
                settle()
                for b in range(2):
                    do(v.scalar_tensor_tensor(y[b][:, 2:], u[b][:, 0:SEQ - 2], tap(CONV - 3, m + b), y[b][:, 2:], ALU.mult, ALU.add))
                settle()
                for b in range(2):
                    do(v.tensor_tensor(B[b], B[b], y[b], ALU.mult))
                settle()
                inner_operands(m, 0)
                split(c % 2)

            two_pairs("ffn_norm1")
            ffn(None)

            v.wait_ge(ident_made, 1)
            v.wait_ge(drained[0], T.add("b0"))
            do(v.reciprocal(query_scale[:, :], token_rms[:, :]))
            settle()
            for j in range(TOK):
                ins = v.tensor_scalar(work[:, j * P:(j + 1) * P], ident[:, :], query_scale[:, j:j + 1], None, ALU.mult)
                if j < TOK - 1:
                    do(ins)
                else:
                    ins.then_inc(token_scales, 1)
            v.wait_ge(rms_spread, 1)
            for m in range(KD):
                v.scalar_tensor_tensor(tile(xT, m), tile(xT, m), gain("final_norm", m), bank[1][:, :], ALU.mult, ALU.mult).then_inc(y_ready, 1)


def columns(w, cols):
    return w.reshape(-1, P, w.shape[1])[:, :, cols].transpose(1, 0, 2).reshape(P, -1)


def weight_stream(w):
    def span(c0, n=2 * P):
        return list(range(c0, c0 + n))

    w_in, uq, ukv = w["mla_w_in"][0], w["mla_w_uq"][0], w["mla_w_ukv"][0]
    yield columns(w_in, span(QRANK))
    yield columns(w_in, span(0))
    yield columns(w_in, span(2 * P))
    rotary = QRANK + KVRANK
    yield columns(w_in, span(rotary, HALF) * 2 + span(rotary + HALF, HALF) * 2)

    def pair(weight, h, parts):
        return columns(weight, [c for at, n in parts for g in (h, h + 1) for c in span(g * sum(n for _, n in parts) + at, n)])

    queries = [pair(uq, h, ((0, NOPE), (NOPE, HALF), (NOPE + HALF, HALF))) for h in range(0, HEADS, 2)]
    latents = [pair(ukv, h, ((0, NOPE), (NOPE, VDIM))) for h in range(0, HEADS, 2)]
    yield from (latents[0], queries[0])
    for q, kv in zip(queries[1:], latents[1:]):
        yield from (q, kv)
    for m in range(KD // 2):
        yield columns(w["mla_w_o"][0], span(m * 2 * P))
    for layer in range(2):
        if layer == 1:
            for m in range(KD // 2):
                for part in range(3):
                    yield columns(w["conv_w_in"][0], span(part * D + m * 2 * P))
            for m in range(KD // 2):
                yield columns(w["conv_w_out"][0], span(m * 2 * P))
        for f in range(KF // 2):
            yield columns(w["ffn_w_gate"][layer], span(f * 2 * P))
            yield columns(w["ffn_w_up"][layer], span(f * 2 * P))
        for m in range(KD // 2):
            for ks in DOWN_K:
                yield columns(w["ffn_w_down"][layer][ks[0] * P:(ks[-1] + 1) * P], span(m * 2 * P))


def kernel(**inputs):
    import concourse.bacc as bacc
    from concourse.bass_utils import run_bass_kernel_spmd

    w = {name: np.asarray(a) for name, a in inputs.items()}
    chunks = list(weight_stream(w))
    weights = np.zeros((len(chunks), P, SLOT), np.float32)
    for c, chunk in enumerate(chunks):
        weights[c, :, :chunk.shape[1]] = chunk
    rows = [w["mla_norm"], w["mla_g_cq"], w["mla_g_ckv"], w["ffn_norm"][0:1], w["conv_norm"], w["ffn_norm"][1:2],
            w["final_norm"][None], w["conv_w"][0]]
    freq = np.float32(1) / np.power(10000.0, np.arange(0, ROPE, 2) / ROPE).astype(np.float32)
    constants = np.stack([np.tile(freq, P // HALF), np.repeat([1, -1], P // 2), np.full(P, math.pi / 2),
                          np.tile(np.repeat([1, 0], HALF), 2), np.tile(np.repeat([0, 1], HALF), 2)])
    constants = constants.astype(np.float32)
    vectors = np.concatenate([r.reshape(-1, P) for r in rows] + [constants]).T
    arrays = {
        "xt": np.ascontiguousarray(w["x"][0].T),
        "positions": w["positions"],
        "vectors": np.ascontiguousarray(vectors),
        "weights_in": weights,
    }
    nc = bacc.Bacc("TRN2", target_bir_lowering=False, num_devices=1)
    args = {n: nc.dram_tensor(n, a.shape, mybir.dt.from_np(a.dtype), kind="ExternalInput").ap() for n, a in arrays.items()}
    out = nc.dram_tensor("out", (D, SEQ), F32, kind="ExternalOutput").ap()
    build(nc, **args, out=out)
    result = run_bass_kernel_spmd(nc, [arrays], core_ids=[0])
    return np.ascontiguousarray(result.results[0]["out"].T)[None]
```

```python
from collections import Counter
from contextlib import ExitStack, contextmanager
import math

import numpy as np

import concourse.bass as bass
from concourse import mybir

F32 = mybir.dt.float32
F32R = mybir.dt.float32r
I32 = mybir.dt.int32
ALU = mybir.AluOpType
ACT = mybir.ActivationFunctionType
AX_X = mybir.AxisListType.X
ds = bass.ds

P = 128
SEQ = 512
TOK = SEQ // P
D = 1024
KD = D // P
HEADS, NOPE, ROPE, VDIM = 8, 128, 64, 128
QRANK, KVRANK = 512, 256
KQ, KKV = QRANK // P, KVRANK // P
D_FF = (8 * D // 3 + 255) // 256 * 256
KF = D_FF // P
CONV = 3
EPS = 1e-6
SCALE = 1.0 / math.sqrt(NOPE + ROPE)
HALF = ROPE // 2
SLOT = KD * 2 * P
PAIRS = HEADS // 2
DOWN_K = [range(0, 8), range(8, 16), range(16, KF)]
UQ_N = KQ * 2 * (NOPE + ROPE)
UKV_N = KKV * 2 * (NOPE + VDIM)
KR_N = KD * 2 * ROPE
DOWN_N = [len(ks) * 2 * P for ks in DOWN_K]
DOWN_AHEAD = (DOWN_N * 3)[2:8]

VEC_ROWS = [("mla_norm", KD), ("mla_g_cq", KQ), ("mla_g_ckv", KKV), ("ffn_norm0", KD), ("conv_norm", KD),
            ("ffn_norm1", KD), ("final_norm", KD), ("conv_w", CONV * KD)]
VEC = {}
for _name, _rows in VEC_ROWS:
    VEC[_name] = sum(r for _, r in VEC_ROWS[:len(VEC)])
N_VEC = sum(r for _, r in VEC_ROWS)
FREQ, SIGN, HALF_PI, HEAD_MASK = N_VEC, N_VEC + 1, N_VEC + 2, N_VEC + 3
N_COLS = N_VEC + 5

PT_STEP = 3 * P
QN, QR = 0, 2 * SEQ
KN = QR + SEQ
VV = KN + 2 * SEQ
PT = [VV + TOK * 2 * VDIM, VV + TOK * 2 * VDIM + TOK * PT_STEP + P]
OO = PT[1] + TOK * PT_STEP + P
CKV = OO + (HEADS - KKV) * SEQ
MASK_Q = OO + HEADS * SEQ
MASK_K = MASK_Q + P
assert MASK_K + P <= KF * SEQ
PI_BELOW = 3.1415925
ROUND = 1.5 * 2.0 ** 23
WARM_UP = 20
MASKED = -float(2.0 ** 93)

Q_BANKS, K_BANKS, V_BANKS, TURNED, HEAD_BANKS = (4, 5, 6), (1, 2), (4, 5), ((7, 0, 7, 0), (7, 0, 6, 0)), (3, 7)
W_O_BANKS, DOWN_BANKS, CONV_OUT_BANKS = ((4, 5), (2, 6)), ((4, 5), (6, 7)), ((0, 1), (2, 3))
ROUND_USES = dict(b0=6, b1=3, b2=3, b3=3, b4=2, b5=2, b6=2, b7=4)

PROB = [[h * 1280 + x for x in (0, 128, 384, 768)] for h in range(2)]


def two_pi_parts():
    rest, parts = 2 * math.pi, []
    for _ in range(2):
        exponent = math.floor(math.log2(rest))
        unit = 2.0 ** (exponent - 11)
        parts.append(math.floor(rest / unit) * unit)
        rest -= parts[-1]
    return parts + [rest]


class Tally:

    def __init__(self):
        self.base, self.here, self.per, self.i = Counter(), Counter(), {}, None

    def add(self, name, k=1):
        self.here[name] += k
        return self.now(name)

    def now(self, name):
        n = self.base[name] + self.here[name]
        per = self.per.get(name, 0)
        return n if self.i is None or not per else self.i * per + n

    @contextmanager
    def loop(self, engine, rounds, **per):
        self.base, self.here = self.base + self.here, Counter()
        with engine.Fori(0, rounds) as i:
            self.per, self.i = per, i
            yield i
            assert dict(+self.here) == per, (dict(self.here), per)
        self.base += Counter({k: v * rounds for k, v in per.items()})
        self.here, self.per, self.i = Counter(), {}, None


def wait(engine, semaphore, count):
    if not (isinstance(count, int) and count == 0):
        engine.wait_ge(semaphore, count)


def turned_view(t, h, qi):
    c0 = PT[h] + qi * P
    return t[:, c0:c0 + TOK * PT_STEP].rearrange("p (j c) -> p j c", j=TOK)[:, 0:qi + 1, 0:P]


def build(nc, xt, positions, vectors, weights_in, out):
    with ExitStack() as ctx:
        def sb(name, cols, dt=F32):
            return ctx.enter_context(nc.sbuf_tensor(name, [P, cols], dt))

        def sem(name):
            return ctx.enter_context(nc.semaphore(name))

        xT = sb("xT", KD * SEQ)
        a_hi, a_lo = sb("a_hi", KD * SEQ, F32R), sb("a_lo", KD * SEQ, F32R)
        mid_hi, mid_lo = sb("mid_hi", KF * SEQ, F32R), sb("mid_lo", KF * SEQ, F32R)
        raw = [sb(f"raw{s}", SLOT) for s in range(2)]
        w_hi = [sb(f"w_hi{s}", SLOT, F32R) for s in range(2)]
        w_lo = [sb(f"w_lo{s}", SLOT, F32R) for s in range(2)]
        work = sb("work", 6 * SEQ)
        cos, sin = sb("cos", SEQ), sb("sin", SEQ)
        rstd = sb("rstd", SEQ)
        acc = sb("acc", SEQ)
        sq = sb("sq", SEQ)
        ident, ones = sb("ident", P), sb("ones", P)
        vec = sb("vec", N_COLS)
        row_max, exp_bias, row_sum, row_inv = (sb(n, 8) for n in ("row_max", "exp_bias", "row_sum", "row_inv"))
        token_rms = sb("token_rms", TOK)
        query_scale = sb("query_scale", TOK)
        eps = sb("eps", 1)
        bank = [ctx.enter_context(nc.psum_tensor(f"bank{b}", [P, SEQ], F32)) for b in range(8)]
        A, MID = (a_hi, a_lo), (mid_hi, mid_lo)
        LATENT = tuple(t[:, CKV:CKV + KKV * SEQ] for t in MID)
        HEAD_OUT = tuple(t[:, OO:OO + HEADS * SEQ] for t in MID)

        def tile(t, m, n=SEQ):
            return t[:, m * SEQ:m * SEQ + n]

        x_squares = [acc[:, :]] + [tile(work, m) for m in range(6)] + [sq[:, :]]
        query_squares = [acc[:, :], tile(work, 4), rstd[:, :], tile(work, 3)]

        def gain(name, m):
            return vec[:, ds(m + VEC[name], 1)] if not isinstance(m, int) else vec[:, VEC[name] + m:VEC[name] + m + 1]

        SWAPPED = ((slice(0, ROPE), slice(ROPE, P)), (slice(ROPE, P), slice(0, ROPE)))

        def tap(t, m):
            return vec[:, VEC["conv_w"] + t * KD + m:VEC["conv_w"] + t * KD + m + 1]

        def turned_bank(h, qi):
            return bank[TURNED[h][qi]][:, 0:(qi + 1) * P].rearrange("p (j c) -> p j c", c=P)

        x_loaded = [sem(f"x_loaded{m}") for m in range(KD)]
        positions_loaded, vectors_loaded = sem("positions_loaded"), sem("vectors_loaded")
        raw_loaded = [sem(f"raw_loaded{s}") for s in range(2)]
        half_loaded, half_hi, half_split = sem("half_loaded"), sem("half_hi"), sem("half_split")
        hi_split = [sem(f"hi_split{s}") for s in range(2)]
        w_split = [sem(f"w_split{s}") for s in range(2)]
        chunk_done = [sem(f"chunk_done{s}") for s in range(2)]
        drained = [sem(f"drained{b}") for b in range(8)]
        operand_ready = sem("operand_ready")
        hi_taken = sem("hi_taken")
        x_squared = sem("x_squared")
        squared = sem("squared")
        taps_started = sem("taps_started")
        x_squares_added = sem("x_squares_added")
        query_squares_added = sem("query_squares_added")
        squares_added = sem("squares_added")
        stat_summed = sem("stat_summed")
        latent_scaled = sem("latent_scaled")
        key_scaled = sem("key_scaled")
        key_rotated = sem("key_rotated")
        rotated = sem("rotated")
        token_scales = sem("token_scales")
        tile_summed = sem("tile_summed")
        rms_spread = sem("rms_spread")
        rms_done = sem("rms_done")
        silu_done = sem("silu_done")
        angles_ready, trig_done = sem("angles_ready"), sem("trig_done")
        masks_made, ones_made, ident_made = sem("masks_made"), sem("ones_made"), sem("ident_made")
        keys_done = sem("keys_done")
        rope_ready = sem("rope_ready")
        scores_done = sem("scores_done")
        max_ready = sem("max_ready")
        rotary_done = sem("rotary_done")
        inverse_ready = sem("inverse_ready")
        probs_ready = sem("probs_ready")
        probs_turned = sem("probs_turned")
        head_done = sem("head_done")
        y_ready = sem("y_ready")
        out_stored = sem("out_stored")
        step = sem("step")
        own = sem("own")

        block = ctx.enter_context(nc.Block())

        @block.sync
        def _(sp):
            T = Tally()
            def load_x(m):
                sp.dma_start(tile(xT, m), xt[m * P:(m + 1) * P, :]).then_inc(x_loaded[m], 16)

            def load(s, c, n=SLOT):
                wait(sp, w_split[s], T.add(f"slot{s}") - 1)
                sp.dma_start(raw[s][:, 0:n].rearrange("p (o n) -> p o n", o=1),
                             weights_in[ds(c, 1), :, 0:n].rearrange("o p n -> p o n")).then_inc(raw_loaded[s], 16)

            def loads(c0, rounds, sizes):
                per = len(sizes)
                with T.loop(sp, rounds, slot0=per // 2, slot1=per // 2) as i:
                    for k, n in enumerate(sizes):
                        load(k % 2, i * per + (c0 + k), n)
                return c0 + rounds * per

            sp.dma_start(vec[:, :], vectors).then_inc(vectors_loaded, 16)
            sp.dma_start(raw[0][:, 0:SLOT // 2], weights_in[0, :, 0:SLOT // 2]).then_inc(half_loaded, 16)
            load_x(0)
            load_x(1)
            T.add("slot0")
            sp.dma_start(raw[0][:, SLOT // 2:], weights_in[0, :, SLOT // 2:]).then_inc(raw_loaded[0], 16)
            for m in range(2, KD):
                load_x(m)
            for c, n in enumerate([SLOT, SLOT, SLOT, KR_N, UKV_N, UQ_N]):
                if c > 0:
                    load(c % 2, c, n)
            c = loads(6, PAIRS - 1, [UQ_N, UKV_N])
            c = loads(c, 2, [SLOT] * 2)
            for layer in range(2):
                c = loads(c, KF // 2, [SLOT] * 2)
                c = loads(c, 2, DOWN_N * 2)
                if layer == 0:
                    c = loads(c, 8, [SLOT] * 2)
            for m in range(KD):
                sp.wait_ge(y_ready, m + 1)
                sp.dma_start(out[m * P:(m + 1) * P, :], tile(xT, m)).then_inc(out_stored, 16)
            sp.wait_ge(out_stored, 16 * KD)

        @block.gpsimd
        def _(pool):
            pool.dma_start(sin[:, :].bitcast(I32), positions.partition_broadcast(P)).then_inc(positions_loaded, 16)
            n = [0]

            def do(instruction):
                instruction.then_inc(own, 1)
                n[0] += 1
                pool.wait_ge(own, n[0])

            def sum_squares(squares, written, before, summed):
                for m in range(1, len(squares)):
                    pool.wait_ge(written, before + m + 1)
                    add = pool.tensor_tensor(acc[:, :], acc[:, :], squares[m], ALU.add)
                    if m < len(squares) - 1:
                        do(add)
                    else:
                        add.then_inc(summed, 1)

            sum_squares(x_squares, x_squared, 0, x_squares_added)
            do(pool.memset(ident[:, :], 0.0))
            pool.affine_select(out=ident[:, :], in_=ident[:, :], compare_op=ALU.not_equal, fill=1.0, base=0,
                               pattern=[[-1, P]], channel_multiplier=1).then_inc(ident_made, 1)

            key, turned_key, part = tile(work, 0), tile(work, 1), tile(work, 2)
            pool.wait_ge(trig_done, 3)
            pool.wait_ge(drained[0], 2)
            pool.wait_ge(squared, KKV + 3)
            for to, of in SWAPPED:
                do(pool.tensor_tensor(part[to, :], key[of, :], sin[of, :], ALU.mult))
            pool.wait_ge(key_scaled, 1)
            pool.tensor_tensor(turned_key, turned_key, part, ALU.add).then_inc(key_rotated, 1)
            sum_squares(query_squares, squared, KKV, query_squares_added)

        @block.tensor
        def _(pe):
            T = Tally()

            def open_bank(b):
                wait(pe, drained[b], T.add(f"b{b}") - 1)

            def taken(b):
                pe.wait_ge(drained[b], T.now(f"b{b}"))

            def product(o, lhs, rhs, start, stop):
                pe.matmul(o, lhs[0], rhs[0], start=start, stop=False, skip_group_check=True)
                pe.matmul(o, lhs[0], rhs[1], start=False, stop=False, skip_group_check=True)
                return pe.matmul(o, lhs[1], rhs[0], start=False, stop=stop, skip_group_check=True)

            def slot(s, c0):
                return w_hi[s][:, c0:c0 + P], w_lo[s][:, c0:c0 + P]

            def operand(buf, k):
                return tile(buf[0], k), tile(buf[1], k)

            def chunk(s, banks, buf, ks=range(KD), first=True, last=True, ready=None, n0=0):
                pe.wait_ge(w_split[s], T.add(f"slot{s}"))
                if first:
                    for b in banks:
                        open_bank(b)
                k_tiles(s, banks, buf, ks, first, last, ready, n0).then_inc(chunk_done[s], 1)

            def k_tiles(s, banks, buf, ks, first, last, ready=None, n0=0):
                for n, k in enumerate(ks):
                    if ready is not None:
                        pe.wait_ge(operand_ready, ready + k + 1)
                    for m, b in enumerate(banks):
                        mm = product(bank[b][:, :], slot(s, ((n0 + n) * len(banks) + m) * P), operand(buf, k),
                                     first and n == 0, last and n == len(ks) - 1)
                return mm

            def stat(b, tiles):
                if tiles:
                    pe.wait_ge(squares_added, T.add("added", tiles))
                open_bank(b)
                pe.matmul(bank[b][:, :], ones[:, :], acc[:, :], start=True, stop=True).then_inc(stat_summed, 1)

            def token_stat(b, tiles):
                if tiles:
                    pe.wait_ge(squares_added, T.add("added", tiles))
                open_bank(b)
                for j in range(TOK):
                    mm = pe.matmul(bank[b][:, j:j + 1], acc[:, j * P:(j + 1) * P], ones[:, 0:1], start=True, stop=True)
                mm.then_inc(stat_summed, 1)

            def spread(b, diagonals):
                open_bank(b)
                for j in range(TOK):
                    pe.wait_ge(token_scales, T.add("scales"))
                    mm = pe.matmul(bank[b][:, j * P:(j + 1) * P], ones[:, :], diagonals[:, j * P:(j + 1) * P], start=True, stop=True)
                mm.then_inc(rms_spread, 1)

            pe.wait_ge(ones_made, 1)
            for _ in range(WARM_UP):
                pe.matmul(bank[7][:, 0:P], ones[:, :], ones[:, :], start=True, stop=True)

            pe.wait_ge(half_split, 1)
            k_tiles(0, [0, 1], A, range(KD // 2), True, False, 0)
            chunk(0, [0, 1], A, range(KD // 2, KD), False, True, 0, n0=KD // 2)
            T.add("b0")
            T.add("b1")
            pe.wait_ge(x_squares_added, 1)
            stat(7, 0)
            chunk(1, [2, 3], A)
            pe.wait_ge(w_split[0], T.add("slot0"))
            open_bank(4)
            open_bank(5)
            k_tiles(0, [4, 5], A, range(KD // 2), True, False)
            token_stat(6, KKV - 1)
            k_tiles(0, [4, 5], A, range(KD // 2, KD), False, True, n0=KD // 2).then_inc(chunk_done[0], 1)
            spread(7, sq)
            chunk(1, [0], A)
            made = KD

            def key(s, h):
                b = K_BANKS[h]
                open_bank(b)
                for k in range(KKV):
                    mm = product(bank[b][:, :], slot(s, (k * 4 + h) * P), operand(LATENT, k), k == 0, k == KKV - 1)
                if h == 1:
                    mm.then_inc(keys_done, 1)

            def query(s, m, ready=None):
                b = Q_BANKS[m]
                open_bank(b)
                for k in range(KQ):
                    if ready is not None:
                        pe.wait_ge(operand_ready, ready + k + 1)
                    mm = product(bank[b][:, :], slot(s, (k * 3 + m) * P), operand(A, k), k == 0, k == KQ - 1)
                if m == 2:
                    mm.then_inc(rotary_done, 1)
                if m == 1:
                    mm.then_inc(chunk_done[s], 1)

            def values(s):
                for j in range(TOK):
                    b = V_BANKS[j // 2]
                    if j % 2 == 0:
                        open_bank(b)
                    for k in range(KKV):
                        c = tuple(t[:, k * SEQ + j * P:k * SEQ + (j + 1) * P] for t in LATENT)
                        wv = tuple(t[:, (k * 4 + 2) * P:(k * 4 + 4) * P] for t in (w_hi[s], w_lo[s]))
                        mm = product(bank[b][:, j % 2 * 2 * VDIM:(j % 2 + 1) * 2 * VDIM], c, wv, k == 0, k == KKV - 1)
                mm.then_inc(chunk_done[s], 1)

            def scores():
                queries = [T.now("b4") - 1, T.now("b5") - 1]
                pe.wait_ge(rope_ready, T.add("rope"))
                for h in range(2):
                    pe.wait_ge(drained[Q_BANKS[h]], queries[h])
                    if h == 0:
                        taken(K_BANKS[0])
                        taken(K_BANKS[1])
                    for qi in range(TOK):
                        L = (qi + 1) * P
                        open_bank(qi)
                        o = bank[qi][:, 0:L]
                        qn = tuple(t[:, QN + h * SEQ + qi * P:QN + h * SEQ + (qi + 1) * P] for t in MID)
                        qr = tuple(t[:, QR + qi * P:QR + (qi + 1) * P] for t in MID)
                        product(o, qn, tuple(t[:, KN + h * SEQ:KN + h * SEQ + L] for t in MID), True, False)
                        product(o, qr, tuple(tile(t, KQ + KKV + h, L) for t in A), False, False)
                        pe.matmul(bank[qi][:, L - P:L], mid_hi[:, MASK_Q:MASK_Q + P], mid_hi[:, MASK_K:MASK_K + P],
                                  start=False, stop=True, skip_group_check=True).then_inc(scores_done, 1)

            def turn(h, tiles):
                for qi in tiles:
                    pe.wait_ge(probs_ready, T.add("probs"))
                    b = TURNED[h][qi]
                    open_bank(b)
                    for j in range(qi + 1):
                        p0 = PROB[h][qi] + j * P
                        tr = pe.transpose(bank[b][:, j * P:(j + 1) * P], work[:, p0:p0 + P], ident[:, :])
                    tr.then_inc(probs_turned, 1)
                return [(TURNED[h][qi], T.now(f"b{TURNED[h][qi]}")) for qi in tiles]

            def heads(turned, values_taken):
                for b, n in values_taken:
                    pe.wait_ge(drained[b], n)
                for h, o in enumerate(HEAD_BANKS):
                    for b, n in turned[h]:
                        pe.wait_ge(drained[b], n)
                    open_bank(o)
                    for j in range(TOK):
                        v0, p0, n = VV + (j * 2 + h) * VDIM, PT[h] + j * SEQ, SEQ - j * P
                        mm = product(bank[o][:, j * P:], tuple(t[:, v0:v0 + VDIM] for t in MID),
                                     tuple(t[:, p0:p0 + n] for t in MID), j == 0, j == TOK - 1)
                    mm.then_inc(head_done, 1)

            pe.wait_ge(w_split[0], T.add("slot0"))
            pe.wait_ge(operand_ready, made + KKV)
            made += KKV
            key(0, 0)
            key(0, 1)
            values(0)
            pe.wait_ge(w_split[1], T.add("slot1"))
            query(1, 2, ready=made)
            query(1, 0)
            query(1, 1)
            pe.wait_ge(query_squares_added, 1)
            token_stat(7, 0)
            pe.wait_ge(operand_ready, made + KQ + 2)
            made += KQ + 2
            pe.wait_ge(masks_made, 1)
            pe.wait_ge(ident_made, 1)
            taken(4)
            taken(5)

            with T.loop(pe, PAIRS - 1, slot0=1, slot1=1, rope=1, probs=8, **ROUND_USES):
                values_taken = [(b, T.now(f"b{b}")) for b in V_BANKS]
                scores()
                pe.wait_ge(w_split[0], T.add("slot0"))
                query(0, 2)
                turn(0, (0, 1))
                query(0, 0)
                turned0 = turn(0, (2, 3))
                query(0, 1)
                turned1 = turn(1, (0, 1))
                pe.wait_ge(w_split[1], T.add("slot1"))
                key(1, 0)
                turned1 += turn(1, (2, 3))
                key(1, 1)
                heads((turned0, turned1), values_taken)
                values(1)
            values_taken = [(b, T.now(f"b{b}")) for b in V_BANKS]
            scores()

            def output(s, m, ks):
                b = W_O_BANKS[s][m]
                if ks[0] == 0:
                    open_bank(b)
                for k in ks:
                    mm = product(bank[b][:, :], slot(s, (k * 2 + m) * P), operand(HEAD_OUT, k), k == 0, k == HEADS - 1)
                return mm

            early, half = range(HEADS - 2), (HEADS - 2) // 2
            pe.wait_ge(w_split[0], T.add("slot0"))
            output(0, 0, early)
            turn(0, (0, 1))
            output(0, 1, early)
            turned0 = turn(0, (2, 3))
            pe.wait_ge(w_split[1], T.add("slot1"))
            output(1, 0, early[:half])
            turned1 = turn(1, (0, 1))
            output(1, 0, early[half:])
            turned1 += turn(1, (2, 3))
            heads((turned0, turned1), values_taken)
            output(1, 1, early[:half])
            for b in HEAD_BANKS:
                taken(b)
            last_two = range(HEADS - 2, HEADS)
            output(0, 0, last_two)
            output(0, 1, last_two).then_inc(chunk_done[0], 1)
            output(1, 1, early[half:])
            output(1, 0, last_two)
            output(1, 1, last_two).then_inc(chunk_done[1], 1)
            for s in range(2):
                chunk(s, W_O_BANKS[s], HEAD_OUT)

            def two_pairs(buf, ready=None):
                with T.loop(pe, 2, slot0=1, slot1=1, b0=1, b1=1, b2=1, b3=1):
                    chunk(0, [0, 1], buf, ready=ready)
                    chunk(1, [2, 3], buf)

            def ffn(made):
                chunk(0, [0, 1], A, ready=made)
                stat(4, KD)
                chunk(1, [2, 3], A)
                with T.loop(pe, KF // 2 - 1, slot0=1, slot1=1, b0=1, b1=1, b2=1, b3=1):
                    chunk(0, [0, 1], A)
                    chunk(1, [2, 3], A)
                made += KD
                with T.loop(pe, 2, slot0=3, slot1=3, b4=1, b5=1, b6=1, b7=1):
                    for c in range(6):
                        banks, ks = DOWN_BANKS[c // 3], DOWN_K[c % 3]
                        if c % 3 < 2:
                            chunk(c % 2, banks, MID, ks, c % 3 == 0, False, ready=made if c < 3 else None)
                        else:
                            pe.wait_ge(w_split[c % 2], T.add(f"slot{c % 2}"))
                            for m, b in enumerate(banks):
                                for n, k in enumerate(ks):
                                    if c < 3 and m == 0:
                                        pe.wait_ge(operand_ready, made + k + 1)
                                    mm = product(bank[b][:, :], slot(c % 2, (n * 2 + m) * P), operand(MID, k), False, k == KF - 1)
                                mm.then_inc((tile_summed, chunk_done[c % 2])[m], 1)
                return made + KF

            made = ffn(made)
            for c in range(12):
                chunk(c % 2, [2 * (c % 3), 2 * (c % 3) + 1], A, ready=made if c == 0 else None)
                if c == 0:
                    stat(6, KD)
            made += KD
            two_pairs(MID, made)
            made += KD
            made = ffn(made)
            token_stat(0, KD)
            spread(1, work)

        @block.scalar
        def _(act):
            T = Tally()

            def split(s, n=SLOT):
                k = T.add(f"slot{s}")
                act.wait_ge(raw_loaded[s], k * 16)
                wait(act, chunk_done[s], k - 1)
                act.activation(w_hi[s][:, 0:n], raw[s][:, 0:n], ACT.Copy).then_inc(hi_split[s], 1)

            def rms(b, width):
                act.wait_ge(stat_summed, T.add("stat"))
                act.activation(bank[b][:, :], bank[b][:, :], ACT.Sqrt, bias=eps[:, 0:1], scale=1.0 / width).then_inc(rms_done, 1)

            def token_rms_of(b, width):
                act.wait_ge(stat_summed, T.add("stat"))
                act.activation(token_rms[:, :], bank[b][:, 0:TOK], ACT.Sqrt, bias=eps[:, 0:1], scale=1.0 / width).then_inc(drained[b], 1)

            def take(dst, src, scale=1.0):
                act.activation(dst, src, ACT.Copy, scale=scale).then_inc(hi_taken, 1)

            def square(src, dst, ring):
                if ring:
                    wait(act, squares_added, max(0, T.add("added") - ring))
                act.activation(dst, src, ACT.Square).then_inc(squared, 1)

            def banks_used(uses):
                for b, n in uses.items():
                    T.add(b, n)

            def square_drained(b, src, dst, ring):
                act.wait_ge(drained[b], T.add(f"b{b}"))
                square(src, dst, ring)

            def take_x(ms):
                for m in ms:
                    act.wait_ge(x_loaded[m], 16)
                    take(tile(a_hi, m), tile(xT, m), gain("mla_norm", m))
                    act.activation(x_squares[m], tile(xT, m), ACT.Square).then_inc(x_squared, 1)

            act.wait_ge(half_loaded, 16)
            act.activation(w_hi[0][:, 0:SLOT // 2], raw[0][:, 0:SLOT // 2], ACT.Copy).then_inc(half_hi, 1)
            act.wait_ge(vectors_loaded, 16)
            take_x(range(2))
            T.add("slot0")
            act.wait_ge(raw_loaded[0], 16)
            act.activation(w_hi[0][:, SLOT // 2:], raw[0][:, SLOT // 2:], ACT.Copy).then_inc(hi_split[0], 1)
            take_x(range(2, KD))
            split(1)
            act.wait_ge(ones_made, 1)
            rms(7, D)
            split(0)
            square_drained(0, tile(work, KQ), acc[:, :], 0)
            square_drained(1, tile(work, KQ + 1), sq[:, :], 1)
            split(1, KR_N)
            act.wait_ge(angles_ready, 1)
            act.activation(sin[:, :], cos[:, :], ACT.Sin, scale=vec[:, SIGN:SIGN + 1]).then_inc(trig_done, 1)
            act.activation(cos[:, :], cos[:, :], ACT.Abs).then_inc(trig_done, 1)
            act.wait_ge(trig_done, 2)
            act.activation(cos[:, :], cos[:, :], ACT.Sin, bias=vec[:, HALF_PI:HALF_PI + 1], scale=-1.0).then_inc(trig_done, 1)
            token_rms_of(6, KVRANK)
            act.wait_ge(latent_scaled, 1)
            take(tile(LATENT[0], 0), tile(work, KQ))
            T.add("b7")
            act.wait_ge(drained[7], T.add("b7"))
            take(tile(LATENT[0], 1), tile(work, KQ + 1))
            split(0, UKV_N)
            split(1, UQ_N)
            act.wait_ge(chunk_done[1], T.now("slot1") - 1)
            for m in range(KQ):
                act.wait_ge(drained[2 + m], T.add(f"b{2 + m}"))
                take(tile(a_hi, m), tile(work, m), gain("mla_g_cq", m))
            act.wait_ge(operand_ready, KD + KKV)
            for m in range(2):
                square(tile(work, m), query_squares[m], 0)
            banks_used(dict(b0=1, b6=1))

            def keys():
                act.wait_ge(keys_done, T.add("keys"))
                for h, b in enumerate(K_BANKS):
                    take(tile(mid_hi[:, KN:], h), bank[b][:, :])

            def queries(s):
                act.wait_ge(chunk_done[s], T.now(f"slot{s}"))
                for h in range(2):
                    take(tile(mid_hi[:, QN:], h), bank[Q_BANKS[h]][:, :])

            def values(s):
                act.wait_ge(chunk_done[s], T.now(f"slot{s}"))
                for h, b in enumerate(V_BANKS):
                    take(tile(mid_hi[:, VV:], h), bank[b][:, :])

            def exps(h):
                for qi in range(TOK):
                    act.wait_ge(max_ready, T.add("max"))
                    k, L = h * TOK + qi, (qi + 1) * P
                    act.activation(work[:, PROB[h][qi]:PROB[h][qi] + L], bank[qi][:, 0:L], ACT.Exp, bias=exp_bias[:, k:k + 1],
                                   scale=query_scale[:, qi:qi + 1], accum_out=row_sum[:, k:k + 1]).then_inc(drained[qi], 1)

            def normalised(h):
                for qi in range(TOK):
                    act.wait_ge(inverse_ready, T.add("inverse"))
                    k, pr = h * TOK + qi, work[:, PROB[h][qi]:PROB[h][qi] + (qi + 1) * P]
                    act.activation(pr, pr, ACT.Copy, scale=row_inv[:, k:k + 1]).then_inc(probs_ready, 1)

            def turned(h, tiles):
                for qi in tiles:
                    act.wait_ge(probs_turned, T.add("turned"))
                    take(turned_view(mid_hi, h, qi), turned_bank(h, qi))

            def rotary_queries():
                act.wait_ge(rotated, T.add("rotated"))
                take(tile(mid_hi[:, QR:], 0), tile(work, 5))

            keys()
            act.wait_ge(drained[0], 2)
            act.wait_ge(operand_ready, KD + KKV + KQ)
            for m in (2, 3):
                square(tile(work, m), query_squares[m], 0)
            values(0)
            act.wait_ge(key_rotated, 1)
            for h in range(2):
                take(tile(a_hi, KQ + KKV + h), tile(work, 1), vec[:, HEAD_MASK + h:HEAD_MASK + h + 1])
            rotary_queries()
            queries(1)
            token_rms_of(7, QRANK)
            split(0, UQ_N)
            banks_used(dict(b1=1, b2=1, b4=2, b5=2, b6=1, b7=1))
            with T.loop(act, PAIRS - 1, slot0=1, slot1=1, keys=1, max=8, inverse=8, turned=8, rotated=1, **ROUND_USES):
                exps(0)
                normalised(0)
                exps(1)
                normalised(1)
                turned(0, (0, 1))
                split(1, UKV_N)
                turned(0, (2, 3))
                turned(1, (0, 1))
                rotary_queries()
                queries(0)
                turned(1, (2, 3))
                keys()
                split(0)
                values(1)
                banks_used(ROUND_USES)
            exps(0)
            normalised(0)
            exps(1)
            normalised(1)
            turned(0, (0, 1))
            split(1)
            turned(0, (2, 3))
            turned(1, range(TOK))
            banks_used(dict(b0=6, b1=2, b2=2, b3=3, b6=1, b7=4))

            def residuals(banks, per, sizes, last=False):
                chunks = KD // 2 * per
                for c in range(chunks):
                    pair = c // per
                    if not last or c < chunks - 2:
                        split(c % 2, sizes[c % len(sizes)])
                    if c % per == per - 1:
                        for h, b in enumerate(banks[pair % len(banks)]):
                            square_drained(b, tile(xT, 2 * pair + h), tile(work, 4 + h), 2)

            def silus():
                act.wait_ge(drained[1], T.add("b1"))
                for b in range(2):
                    act.activation(tile(work, 2 + b), tile(work, b), ACT.Silu).then_inc(silu_done, 1)

            def ffn(last):
                split(0)
                rms(4, D)
                silus()
                split(1)
                with T.loop(act, KF // 2 - 1, slot0=1, slot1=1, b1=1):
                    split(0)
                    silus()
                    split(1)
                banks_used(dict(b0=KF // 2, b2=KF // 2, b3=KF // 2, b4=1))
                residuals(DOWN_BANKS, 3, DOWN_AHEAD, last)

            residuals(W_O_BANKS, 1, [SLOT])
            ffn(False)
            for c in range(12):
                if c % 3 == 2:
                    for b in range(2):
                        act.wait_ge(drained[4 + b], T.add(f"b{4 + b}"))
                        act.activation(tile(work, 2 + b), tile(work, 4 + b), ACT.Copy,
                                       scale=tap(CONV - 1, c // 3 * 2 + b)).then_inc(taps_started, 1)
                split(c % 2)
                if c == 0:
                    rms(6, D)
            banks_used(dict(b0=4, b1=4, b2=4, b3=4, b6=1))
            residuals(CONV_OUT_BANKS, 1, [SLOT])
            ffn(True)
            token_rms_of(0, D)

        @block.vector
        def _(v):
            T = Tally()

            def do(instruction):
                instruction.then_inc(step, 1)
                T.add("step")

            def settle():
                v.wait_ge(step, T.now("step"))

            def drain(b, instruction):
                instruction.then_inc(drained[b], 1)
                T.add(f"b{b}")

            def ready(instruction):
                instruction.then_inc(operand_ready, 1)
                T.add("operand")

            def all_ready():
                v.wait_ge(operand_ready, T.now("operand"))

            def landed(*banks):
                for b in banks:
                    v.wait_ge(drained[b], T.now(f"b{b}"))

            def done(s):
                v.wait_ge(chunk_done[s], T.now(f"slot{s}"))

            def split(s, n=SLOT):
                v.wait_ge(hi_split[s], T.add(f"slot{s}"))
                v.tensor_tensor(w_lo[s][:, 0:n], raw[s][:, 0:n], w_hi[s][:, 0:n], ALU.subtract).then_inc(w_split[s], 1)

            def at(t, m):
                return t[:, ds(m * SEQ, SEQ)]

            def normed(name, ms):
                for m in ms:
                    do(v.tensor_scalar(at(a_hi, m), at(xT, m), gain(name, m), None, ALU.mult))
                settle()
                for m in ms:
                    ready(v.scalar_tensor_tensor(at(a_lo, m), at(xT, m), gain(name, m), at(a_hi, m).bitcast(F32),
                                                 ALU.mult, ALU.subtract))

            def clear_acc():
                wait(v, squares_added, T.now("added"))
                do(v.memset(acc[:, :], 0.0))
                settle()

            def add_squares(buffers):
                for buf in buffers:
                    wait(v, squares_added, T.now("added"))
                    v.wait_ge(squared, T.add("squared"))
                    T.add("added")
                    v.tensor_tensor(acc[:, :], acc[:, :], buf, ALU.add).then_inc(squares_added, 1)

            def inverse_rms(b, dst=None):
                v.wait_ge(rms_done, T.add("rms"))
                if dst is None:
                    do(v.reciprocal(bank[b][:, :], bank[b][:, :]))
                    settle()
                else:
                    drain(b, v.reciprocal(dst[:, :], bank[b][:, :]))
                    landed(b)

            def scaled(m, b):
                drain(b, v.tensor_tensor(tile(work, m), bank[b][:, :], rstd[:, :], ALU.mult))

            def taken():
                v.wait_ge(hi_taken, T.add("taken"))

            def lo(dst, src, hi):
                return v.tensor_tensor(dst, src, hi, ALU.subtract)

            def rotate(dst, tmp, src, b=None):
                do(v.tensor_tensor(dst, src, cos[:, :], ALU.mult))
                for to, of in SWAPPED:
                    part = v.tensor_tensor(tmp[to, :], src[of, :], sin[of, :], ALU.mult)
                    if to.start and b is not None:
                        drain(b, part)
                        landed(b)
                    else:
                        do(part)
                settle()
                v.tensor_tensor(dst, dst, tmp, ALU.add).then_inc(rotated, 1)
                T.add("rotated")

            def diagonals(dst, scale=1.0):
                do(v.reciprocal(query_scale[:, :], token_rms[:, :]))
                settle()
                for j in range(TOK):
                    v.tensor_scalar(dst[:, j * P:(j + 1) * P], ident[:, :], query_scale[:, j:j + 1], None, ALU.mult).then_inc(token_scales, 1)

            v.memset(eps[:, :], EPS)
            v.memset(ones[:, :], 1.0).then_inc(ones_made, 1)
            mask_q, mask_k = (mid_hi[:, c:c + P].bitcast(F32) for c in (MASK_Q, MASK_K))
            v.memset(mask_q[:, 0:P // 2], 1.0)
            v.memset(mask_q[:, P // 2:P], 0.0)
            v.memset(mask_k[:, 0:P // 2], 0.0)
            v.memset(mask_k[:, P // 2:P], MASKED).then_inc(masks_made, 1)

            v.wait_ge(vectors_loaded, 16)
            for m in range(KD):
                if m == 0:
                    v.wait_ge(half_hi, 1)
                    v.tensor_tensor(w_lo[0][:, 0:SLOT // 2], raw[0][:, 0:SLOT // 2], w_hi[0][:, 0:SLOT // 2], ALU.subtract).then_inc(half_split, 1)
                taken()
                ready(v.scalar_tensor_tensor(tile(a_lo, m), tile(xT, m), gain("mla_norm", m), tile(a_hi, m).bitcast(F32),
                                             ALU.mult, ALU.subtract))
                if m == 2:
                    v.wait_ge(hi_split[0], T.add("slot0"))
                    v.tensor_tensor(w_lo[0][:, SLOT // 2:], raw[0][:, SLOT // 2:], w_hi[0][:, SLOT // 2:], ALU.subtract).then_inc(w_split[0], 1)
            split(1)

            angle, turns = cos[:, :], sin[:, :]
            v.wait_ge(positions_loaded, 16)
            do(v.tensor_copy(angle, turns.bitcast(I32)))
            settle()
            do(v.tensor_scalar(angle, angle, vec[:, FREQ:FREQ + 1], None, ALU.mult))
            settle()
            for unit in (2048.0, 1.0):
                do(v.tensor_scalar(turns, angle, 1.0 / (2 * math.pi * unit), ROUND, ALU.mult, ALU.add))
                settle()
                do(v.tensor_scalar(turns, turns, ROUND, None, ALU.subtract))
                settle()
                for part in two_pi_parts():
                    do(v.scalar_tensor_tensor(angle, turns, -part * unit, angle, ALU.mult, ALU.add))
                    settle()
            v.tensor_scalar(angle, angle, PI_BELOW, -PI_BELOW, ALU.min, ALU.max).then_inc(angles_ready, 1)

            split(0)
            inverse_rms(7, rstd)
            scaled(4, 0)
            scaled(5, 1)
            T.add("squared")
            add_squares([sq[:, :]])
            done(1)
            scaled(0, 2)
            scaled(1, 3)
            v.wait_ge(ident_made, 1)
            v.wait_ge(drained[6], T.add("b6"))
            diagonals(sq)
            split(1, KR_N)
            v.wait_ge(rms_spread, 1)
            for t in range(KKV):
                c = tile(work, KQ + t)
                ins = v.scalar_tensor_tensor(c, c, gain("mla_g_ckv", t), bank[7][:, :], ALU.mult, ALU.mult)
                if t == 0:
                    ins.then_inc(latent_scaled, 1)
                else:
                    drain(7, ins)
            done(0)
            scaled(2, 4)
            scaled(3, 5)
            for t in range(KKV):
                taken()
                ready(lo(tile(LATENT[1], t), tile(work, KQ + t), tile(LATENT[0], t)))
            split(0, UKV_N)
            split(1, UQ_N)
            T.add("squared")
            for t in range(KQ):
                taken()
                ready(v.scalar_tensor_tensor(tile(a_lo, t), tile(work, t), gain("mla_g_cq", t), tile(a_hi, t).bitcast(F32),
                                             ALU.mult, ALU.subtract))

            def keys():
                for h, b in enumerate(K_BANKS):
                    taken()
                    drain(b, lo(tile(mid_lo[:, KN:], h), bank[b][:, :], tile(mid_hi[:, KN:], h)))

            def queries():
                for h in range(2):
                    b = Q_BANKS[h]
                    taken()
                    drain(b, lo(tile(mid_lo[:, QN:], h), bank[b][:, :], tile(mid_hi[:, QN:], h)))

            def rotate_queries():
                v.wait_ge(rotary_done, T.add("rope"))
                rotate(tile(work, 5), sq[:, :], bank[Q_BANKS[2]][:, :], b=Q_BANKS[2])

            def rotary_queries():
                taken()
                lo(tile(mid_lo[:, QR:], 0), tile(work, 5), tile(mid_hi[:, QR:], 0)).then_inc(rope_ready, 1)

            def values():
                for h, b in enumerate(V_BANKS):
                    taken()
                    drain(b, lo(tile(mid_lo[:, VV:], h), bank[b][:, :], tile(mid_hi[:, VV:], h)))

            def row_maxima(h):
                for qi in range(TOK):
                    k, L = h * TOK + qi, (qi + 1) * P
                    v.wait_ge(scores_done, T.add("scores"))
                    do(v.tensor_reduce(row_max[:, k:k + 1], bank[qi][:, 0:L], AX_X, ALU.max))
                    settle()
                    v.tensor_scalar(exp_bias[:, k:k + 1], row_max[:, k:k + 1], query_scale[:, qi:qi + 1], -1.0,
                                    ALU.mult, ALU.mult).then_inc(max_ready, 1)

            def inverse_sums(h):
                for qi in range(TOK):
                    k = h * TOK + qi
                    v.wait_ge(drained[qi], T.add(f"b{qi}"))
                    v.reciprocal(row_inv[:, k:k + 1], row_sum[:, k:k + 1]).then_inc(inverse_ready, 1)

            def turned(h, tiles):
                for qi in tiles:
                    taken()
                    drain(TURNED[h][qi], lo(turned_view(mid_lo, h, qi), turned_bank(h, qi), turned_view(mid_hi, h, qi)))

            def heads(o):
                for h, b in enumerate(HEAD_BANKS):
                    v.wait_ge(head_done, T.add("heads"))
                    do(v.tensor_copy(HEAD_OUT[0][:, ds(o + h * SEQ, SEQ)], bank[b][:, :]))
                settle()
                for h, b in enumerate(HEAD_BANKS):
                    hi_t, lo_t = (t[:, ds(o + h * SEQ, SEQ)] for t in HEAD_OUT)
                    drain(b, lo(lo_t, bank[b][:, :], hi_t))

            all_ready()
            v.wait_ge(squared, KKV + 1)
            T.add("squared", KQ - 1)
            scaled(0, 0)
            landed(0)
            v.wait_ge(trig_done, 3)
            v.wait_ge(squared, KKV + 2)
            v.tensor_tensor(tile(work, 1), tile(work, 0), cos[:, :], ALU.mult).then_inc(key_scaled, 1)
            keys()
            values()
            rotate_queries()
            for h in range(2):
                taken()
                own_dims = vec[:, HEAD_MASK + h:HEAD_MASK + h + 1]
                ready(v.scalar_tensor_tensor(tile(a_lo, KQ + KKV + h), tile(work, 1), own_dims,
                                             tile(a_hi, KQ + KKV + h).bitcast(F32), ALU.mult, ALU.subtract))
            rotary_queries()
            queries()
            v.wait_ge(drained[7], T.add("b7"))
            do(v.reciprocal(query_scale[:, :], token_rms[:, :]))
            settle()
            do(v.tensor_scalar(query_scale[:, :], query_scale[:, :], SCALE, None, ALU.mult))
            settle()
            split(0, UQ_N)

            with T.loop(v, PAIRS - 1, slot0=1, slot1=1, taken=15, step=12, scores=8, heads=2, rope=1, rotated=1, **ROUND_USES) as i:
                row_maxima(0)
                inverse_sums(0)
                row_maxima(1)
                inverse_sums(1)
                turned(0, (0, 1))
                split(1, UKV_N)
                turned(0, (2, 3))
                v.wait_ge(rope_ready, T.now("rope"))
                rotate_queries()
                turned(1, (0, 1))
                rotary_queries()
                queries()
                turned(1, (2, 3))
                keys()
                split(0)
                heads(i * (2 * SEQ))
                values()
            row_maxima(0)
            inverse_sums(0)
            row_maxima(1)
            inverse_sums(1)
            turned(0, (0, 1))
            split(1)
            turned(0, (2, 3))
            turned(1, range(TOK))
            heads((HEADS - 2) * SEQ)

            def add_result(b, m):
                drain(b, v.tensor_tensor(at(xT, m), bank[b][:, :], at(xT, m), ALU.add))

            def next_operands(banks, ms, name):
                landed(*banks)
                if name:
                    normed(name, ms)
                add_squares([tile(work, 4), tile(work, 5)])

            def conv_out():
                with T.loop(v, 2, slot0=1, slot1=1, b0=1, b1=1, b2=1, b3=1, step=4, squared=4, added=4, operand=4) as i:
                    for s in range(2):
                        banks, ms = (2 * s, 2 * s + 1), [i * 4 + (2 * s + k) for k in range(2)]
                        done(s)
                        for b, m in zip(banks, ms):
                            add_result(b, m)
                        next_operands(banks, ms, "ffn_norm1")
                        split(s)

            def ffn_round(f, first=False):
                done(0)
                all_ready()
                if first:
                    inverse_rms(4, rstd)
                    clear_acc()
                scaled(0, 0)
                scaled(1, 1)
                split(0)
                for b in range(2):
                    v.wait_ge(silu_done, T.add("silu"))
                    do(v.tensor_tensor(tile(work, 2 + b), tile(work, 2 + b), rstd[:, :], ALU.mult))
                settle()
                all_ready()
                done(1)
                for b in range(2):
                    drain(2 + b, v.tensor_tensor(tile(work, 4 + b), bank[2 + b][:, :], tile(work, 2 + b), ALU.mult))
                landed(2, 3)
                inner_operands(f, 4)
                split(1)

            def inner_operands(f, w):
                for b in range(2):
                    do(v.tensor_copy(at(mid_hi, f + b), tile(work, w + b)))
                settle()
                for b in range(2):
                    ready(lo(at(mid_lo, f + b), tile(work, w + b), at(mid_hi, f + b)))

            def ffn(name):
                ffn_round(0, first=True)
                with T.loop(v, KF // 2 - 1, slot0=1, slot1=1, b0=1, b1=1, b2=1, b3=1, step=4, silu=2, operand=2) as i:
                    ffn_round(i * 2 + 2)

                def down_round(m, last):
                    for c in range(6):
                        if c % 3 == 2:
                            pair = c // 3
                            banks, ms = DOWN_BANKS[pair], [m + (2 * pair + k) for k in range(2)]
                            v.wait_ge(tile_summed, T.add("summed"))
                            add_result(banks[0], ms[0])
                            done(c % 2)
                            add_result(banks[1], ms[1])
                            next_operands(banks, ms, name)
                        if not (last and c >= 4):
                            split(c % 2, DOWN_AHEAD[c])
                if name:
                    with T.loop(v, 2, slot0=3, slot1=3, summed=2, b4=1, b5=1, b6=1, b7=1, step=4, squared=4, added=4, operand=4) as i:
                        down_round(i * 4, False)
                else:
                    down_round(0, False)
                    down_round(4, True)

            clear_acc()
            for c in range(4):
                banks, ms = W_O_BANKS[c % 2], (2 * c, 2 * c + 1)
                done(c % 2)
                for b, m in zip(banks, ms):
                    add_result(b, m)
                if c == 0:
                    split(0)
                next_operands(banks, ms, "ffn_norm0")
                if c > 0:
                    split(c % 2)
            ffn("conv_norm")

            for c in range(12):
                m, part = c // 3 * 2, c % 3
                all_ready()
                done(c % 2)
                if c == 0:
                    inverse_rms(6, rstd)
                    clear_acc()
                B, y, u = ([tile(work, w + b) for b in range(2)] for w in (0, 2, 4))
                if part < 2:
                    scaled(2 * part, 2 * part)
                    scaled(2 * part + 1, 2 * part + 1)
                    split(c % 2)
                if part == 1:
                    landed(2, 3)
                    for b in range(2):
                        do(v.tensor_tensor(y[b], y[b], rstd[:, :], ALU.mult))
                    settle()
                if part < 2:
                    continue
                for b in range(2):
                    drain(4 + b, v.tensor_tensor(u[b], bank[4 + b][:, :], y[b], ALU.mult))
                landed(0, 1, 4, 5)
                for b in range(2):
                    v.wait_ge(taps_started, m + b + 1)
                    do(v.scalar_tensor_tensor(y[b][:, 1:], u[b][:, 0:SEQ - 1], tap(CONV - 2, m + b), y[b][:, 1:], ALU.mult, ALU.add))
                settle()
                for b in range(2):
                    do(v.scalar_tensor_tensor(y[b][:, 2:], u[b][:, 0:SEQ - 2], tap(CONV - 3, m + b), y[b][:, 2:], ALU.mult, ALU.add))
                settle()
                for b in range(2):
                    do(v.tensor_tensor(B[b], B[b], y[b], ALU.mult))
                settle()
                inner_operands(m, 0)
                split(c % 2)

            conv_out()
            ffn(None)

            v.wait_ge(drained[0], T.add("b0"))
            diagonals(work)
            v.wait_ge(rms_spread, 2)
            for m in range(KD):
                v.scalar_tensor_tensor(tile(xT, m), tile(xT, m), gain("final_norm", m), bank[1][:, :], ALU.mult, ALU.mult).then_inc(y_ready, 1)


def columns(w, cols):
    return w.reshape(-1, P, w.shape[1])[:, :, cols].transpose(1, 0, 2).reshape(P, -1)


def weight_stream(w):
    def span(c0, n=2 * P):
        return list(range(c0, c0 + n))

    w_in, uq, ukv = w["mla_w_in"][0], w["mla_w_uq"][0], w["mla_w_ukv"][0]
    yield columns(w_in, span(QRANK))
    yield columns(w_in, span(0))
    yield columns(w_in, span(2 * P))
    rotary = QRANK + KVRANK
    yield columns(w_in, span(rotary, HALF) * 2 + span(rotary + HALF, HALF) * 2)

    def pair(weight, h, parts):
        return columns(weight, [c for at, n in parts for g in (h, h + 1) for c in span(g * sum(n for _, n in parts) + at, n)])

    queries = [pair(uq, h, ((0, NOPE), (NOPE, HALF), (NOPE + HALF, HALF))) for h in range(0, HEADS, 2)]
    latents = [pair(ukv, h, ((0, NOPE), (NOPE, VDIM))) for h in range(0, HEADS, 2)]
    yield from (latents[0], queries[0])
    for q, kv in zip(queries[1:], latents[1:]):
        yield from (q, kv)
    for m in range(KD // 2):
        yield columns(w["mla_w_o"][0], span(m * 2 * P))
    for layer in range(2):
        if layer == 1:
            for m in range(KD // 2):
                for part in range(3):
                    yield columns(w["conv_w_in"][0], span(part * D + m * 2 * P))
            for m in range(KD // 2):
                yield columns(w["conv_w_out"][0], span(m * 2 * P))
        for f in range(KF // 2):
            yield columns(w["ffn_w_gate"][layer], span(f * 2 * P))
            yield columns(w["ffn_w_up"][layer], span(f * 2 * P))
        for m in range(KD // 2):
            for ks in DOWN_K:
                yield columns(w["ffn_w_down"][layer][ks[0] * P:(ks[-1] + 1) * P], span(m * 2 * P))


def kernel(**inputs):
    import concourse.bacc as bacc
    from concourse.bass_utils import run_bass_kernel_spmd

    w = {name: np.asarray(a) for name, a in inputs.items()}
    chunks = list(weight_stream(w))
    weights = np.zeros((len(chunks), P, SLOT), np.float32)
    for c, chunk in enumerate(chunks):
        weights[c, :, :chunk.shape[1]] = chunk
    rows = [w["mla_norm"], w["mla_g_cq"], w["mla_g_ckv"], w["ffn_norm"][0:1], w["conv_norm"], w["ffn_norm"][1:2],
            w["final_norm"][None], w["conv_w"][0]]
    freq = np.float32(1) / np.power(10000.0, np.arange(0, ROPE, 2) / ROPE).astype(np.float32)
    constants = np.stack([np.tile(freq, P // HALF), np.repeat([1, -1], P // 2), np.full(P, math.pi / 2),
                          np.tile(np.repeat([1, 0], HALF), 2), np.tile(np.repeat([0, 1], HALF), 2)])
    constants = constants.astype(np.float32)
    vectors = np.concatenate([r.reshape(-1, P) for r in rows] + [constants]).T
    arrays = {
        "xt": np.ascontiguousarray(w["x"][0].T),
        "positions": w["positions"],
        "vectors": np.ascontiguousarray(vectors),
        "weights_in": weights,
    }
    nc = bacc.Bacc("TRN2", target_bir_lowering=False, num_devices=1)
    args = {n: nc.dram_tensor(n, a.shape, mybir.dt.from_np(a.dtype), kind="ExternalInput").ap() for n, a in arrays.items()}
    out = nc.dram_tensor("out", (D, SEQ), F32, kind="ExternalOutput").ap()
    build(nc, **args, out=out)
    result = run_bass_kernel_spmd(nc, [arrays], core_ids=[0])
    return np.ascontiguousarray(result.results[0]["out"].T)[None]
```
